# Optimizing a Trainium2 kernel written in Bass

```python
import jax, jax.numpy as jnp
from jax import lax
import numpy as np

D_MODEL = 1024
BATCH = 1
SEQ = 512
DEPTH = 2

N_MIXERS = 2
N_GLA = (DEPTH + 1) // 2
N_MLA = DEPTH // 2
EPS = 1e-6

GLA_HEADS = 4
GLA_DK = D_MODEL // 2 // GLA_HEADS
GLA_DV = D_MODEL // GLA_HEADS
GLA_GATE_RANK = 16
GLA_TAU = 16.0
GLA_CHUNK = 64

MLA_HEADS = 8
MLA_NOPE = 128
MLA_ROPE = 64
MLA_VDIM = 128
MLA_Q_RANK = 384
MLA_KV_RANK = 256
ROPE_THETA = 10000.0
Q_BLOCK = 128

D_FF = -(-8 * D_MODEL // (3 * 256)) * 256


def rmsnorm(t, g):
    tf = t.astype(jnp.float32)
    y = tf * lax.rsqrt(jnp.mean(tf * tf, axis=-1, keepdims=True) + EPS)
    return (y * g.astype(jnp.float32)).astype(t.dtype)

def modulate(t, g, shift, scale):
    return rmsnorm(t, g) * (1.0 + scale[:, None, :]) + shift[:, None, :]

def gla_chunked(q, k, v, log_a):
    B, S, H, DK = q.shape
    DV = v.shape[-1]
    C = GLA_CHUNK
    n = S // C

    def to_chunks(t):
        return t.astype(jnp.float32).reshape(B, n, C, H, t.shape[-1]).transpose(1, 0, 3, 2, 4)

    qc, kc, vc, gc = to_chunks(q), to_chunks(k), to_chunks(v), to_chunks(log_a)
    causal = jnp.tril(jnp.ones((C, C), dtype=bool))[:, :, None]

    def step(state, inp):
        qi, ki, vi, gi = inp
        b = jnp.cumsum(gi, axis=-2)
        o_inter = jnp.einsum('bhck,bhkv->bhcv', qi * jnp.exp(b), state)
        diff = b[:, :, :, None, :] - b[:, :, None, :, :]
        decay = jnp.exp(jnp.where(causal, diff, -jnp.inf))
        attn = jnp.einsum('bhik,bhjk,bhijk->bhij', qi, ki, decay)
        o_intra = jnp.einsum('bhij,bhjv->bhiv', attn, vi)
        b_last = b[:, :, -1:, :]
        new_state = state * jnp.exp(b_last[:, :, 0, :])[..., None] + jnp.einsum(
            'bhck,bhcv->bhkv', ki * jnp.exp(b_last - b), vi)
        return new_state, o_inter + o_intra

    state0 = jnp.zeros((B, H, DK, DV), jnp.float32)
    _, o = lax.scan(step, state0, (qc, kc, vc, gc))
    return o.transpose(1, 0, 3, 2, 4).reshape(B, S, H, DV)

def gla_mixer(h, w_in, w_gate, b_gate, g_out, w_out):
    B, S, _ = h.shape
    H, DK, DV = GLA_HEADS, GLA_DK, GLA_DV
    proj = h @ w_in
    q, k, v, r, glr = jnp.split(proj, [H * DK, 2 * H * DK, 2 * H * DK + H * DV,
                                       2 * H * DK + 2 * H * DV], axis=-1)
    q = q.reshape(B, S, H, DK) * (DK ** -0.5)
    k = k.reshape(B, S, H, DK)
    v = v.reshape(B, S, H, DV)
    r = r.reshape(B, S, H, DV)
    log_a = jax.nn.log_sigmoid((glr @ w_gate + b_gate).astype(jnp.float32)) / GLA_TAU
    o = gla_chunked(q, k, v, log_a.reshape(B, S, H, DK)).astype(h.dtype)
    o = rmsnorm(o, g_out) * jax.nn.silu(r)
    return o.reshape(B, S, H * DV) @ w_out

def apply_rope(t, cos, sin):
    tf = t.astype(jnp.float32).reshape(*t.shape[:-1], -1, 2)
    t1, t2 = tf[..., 0], tf[..., 1]
    out = jnp.stack([t1 * cos - t2 * sin, t1 * sin + t2 * cos], axis=-1).reshape(t.shape)
    return out.astype(t.dtype)

def mla_mixer(h, cos, sin, w_in, g_q, w_q_up, g_kv, w_kv_up, w_out):
    B, S, _ = h.shape
    H = MLA_HEADS
    proj = h @ w_in
    cq, ckv, k_rope = jnp.split(proj, [MLA_Q_RANK, MLA_Q_RANK + MLA_KV_RANK], axis=-1)
    q = (rmsnorm(cq, g_q) @ w_q_up).reshape(B, S, H, MLA_NOPE + MLA_ROPE)
    q_nope, q_rope = jnp.split(q, [MLA_NOPE], axis=-1)
    kv = (rmsnorm(ckv, g_kv) @ w_kv_up).reshape(B, S, H, MLA_NOPE + MLA_VDIM)
    k_nope, v = jnp.split(kv, [MLA_NOPE], axis=-1)
    q_rope = apply_rope(q_rope, cos, sin)
    k_rope = apply_rope(k_rope[:, :, None, :], cos, sin)[:, :, 0, :]

    scale = (MLA_NOPE + MLA_ROPE) ** -0.5
    nb = S // Q_BLOCK
    qn = q_nope.reshape(B, nb, Q_BLOCK, H, MLA_NOPE).transpose(1, 0, 2, 3, 4)
    qr = q_rope.reshape(B, nb, Q_BLOCK, H, MLA_ROPE).transpose(1, 0, 2, 3, 4)
    kpos = jnp.arange(S)

    def block(args):
        qn_b, qr_b, idx = args
        s = (jnp.einsum('bqhd,bkhd->bhqk', qn_b, k_nope)
             + jnp.einsum('bqhd,bkd->bhqk', qr_b, k_rope)).astype(jnp.float32) * scale
        qpos = idx * Q_BLOCK + jnp.arange(Q_BLOCK)
        mask = kpos[None, :] <= qpos[:, None]
        p = jax.nn.softmax(jnp.where(mask, s, -jnp.inf), axis=-1)
        return jnp.einsum('bhqk,bkhd->bqhd', p.astype(v.dtype), v)

    o = lax.map(block, (qn, qr, jnp.arange(nb)))
    o = o.transpose(1, 0, 2, 3, 4).reshape(B, S, H * MLA_VDIM)
    return o @ w_out

def swiglu(h, w_in, w_out):
    gate, up = jnp.split(h @ w_in, 2, axis=-1)
    return (jax.nn.silu(gate) * up) @ w_out

def first_inputs(seed: int = 0) -> dict:
    key = jax.random.key(seed)
    ks = jax.random.split(key, 24)
    D = D_MODEL
    f32 = jnp.float32

    def w(k, shape, fan_in):
        return jax.random.normal(k, shape, f32) * (fan_in ** -0.5)

    def gain(k, shape):
        return 1.0 + 0.02 * jax.random.normal(k, shape, f32)

    x = jax.random.normal(ks[0], (BATCH, SEQ, D), f32)
    c = jax.random.normal(ks[1], (BATCH, D), f32)
    offsets = jax.random.randint(ks[2], (BATCH, 1), 0, 4096, dtype=jnp.int32)
    positions = offsets + jnp.arange(SEQ, dtype=jnp.int32)[None, :]

    gla_in = 2 * GLA_HEADS * GLA_DK + 2 * GLA_HEADS * GLA_DV + GLA_GATE_RANK
    mla_in = MLA_Q_RANK + MLA_KV_RANK + MLA_ROPE
    return {
        "x": x,
        "c": c,
        "positions": positions,
        "ada_w": w(ks[3], (DEPTH, D, 6 * D), D),
        "ada_b": 0.02 * jax.random.normal(ks[4], (DEPTH, 6 * D), f32),
        "norm_mix": gain(ks[5], (DEPTH, D)),
        "norm_ffn": gain(ks[6], (DEPTH, D)),
        "gla_w_in": w(ks[7], (N_GLA, D, gla_in), D),
        "gla_w_gate": w(ks[8], (N_GLA, GLA_GATE_RANK, GLA_HEADS * GLA_DK), GLA_GATE_RANK),
        "gla_b_gate": 0.1 * jax.random.normal(ks[9], (N_GLA, GLA_HEADS * GLA_DK), f32),
        "gla_g_out": gain(ks[10], (N_GLA, GLA_DV)),
        "gla_w_out": w(ks[11], (N_GLA, GLA_HEADS * GLA_DV, D), GLA_HEADS * GLA_DV),
        "mla_w_in": w(ks[12], (N_MLA, D, mla_in), D),
        "mla_g_q": gain(ks[13], (N_MLA, MLA_Q_RANK)),
        "mla_w_q_up": w(ks[14], (N_MLA, MLA_Q_RANK, MLA_HEADS * (MLA_NOPE + MLA_ROPE)), MLA_Q_RANK),
        "mla_g_kv": gain(ks[15], (N_MLA, MLA_KV_RANK)),
        "mla_w_kv_up": w(ks[16], (N_MLA, MLA_KV_RANK, MLA_HEADS * (MLA_NOPE + MLA_VDIM)), MLA_KV_RANK),
        "mla_w_out": w(ks[17], (N_MLA, MLA_HEADS * MLA_VDIM, D), MLA_HEADS * MLA_VDIM),
        "ffn_w_in": w(ks[18], (DEPTH, D, 2 * D_FF), D),
        "ffn_w_out": w(ks[19], (DEPTH, D_FF, D), D_FF),
        "final_norm": gain(ks[20], (D,)),
    }

def first_block(x, c, positions, ada_w, ada_b, norm_mix, norm_ffn,
              gla_w_in, gla_w_gate, gla_b_gate, gla_g_out, gla_w_out,
              mla_w_in, mla_g_q, mla_w_q_up, mla_g_kv, mla_w_kv_up, mla_w_out,
              ffn_w_in, ffn_w_out, final_norm):
    inv_freq = ROPE_THETA ** (-jnp.arange(0, MLA_ROPE, 2, dtype=jnp.float32) / MLA_ROPE)
    ang = positions.astype(jnp.float32)[..., None] * inv_freq
    cos = jnp.cos(ang)[:, :, None, :]
    sin = jnp.sin(ang)[:, :, None, :]
    c_act = jax.nn.silu(c)

    for i in range(DEPTH):
        mod = c_act @ ada_w[i] + ada_b[i]
        sh1, sc1, g1, sh2, sc2, g2 = jnp.split(mod, 6, axis=-1)
        h = modulate(x, norm_mix[i], sh1, sc1)
        j = i // N_MIXERS
        if i % N_MIXERS == 0:
            y = gla_mixer(h, gla_w_in[j], gla_w_gate[j], gla_b_gate[j], gla_g_out[j], gla_w_out[j])
        else:
            y = mla_mixer(h, cos, sin, mla_w_in[j], mla_g_q[j], mla_w_q_up[j],
                          mla_g_kv[j], mla_w_kv_up[j], mla_w_out[j])
        x = x + g1[:, None, :] * y
        h = modulate(x, norm_ffn[i], sh2, sc2)
        x = x + g2[:, None, :] * swiglu(h, ffn_w_in[i], ffn_w_out[i])

    return rmsnorm(x, final_norm)


DEPTH_2 = 1

POOL_WIDTH = D_MODEL // 2
POOL_GROUPS = 4
POOL_GROUP_WIDTH = POOL_WIDTH // POOL_GROUPS
POOL_WINDOWS = (2, 4, 8, 16)
CONV_WIDTH = D_MODEL // 2
CONV_KERNEL = 31
N_BRANCHES = 2
IN_WIDTH = POOL_WIDTH + 2 * CONV_WIDTH + N_BRANCHES * D_MODEL
PEER_HEADS = 8
PEER_KEY_DIM = 256
PEER_HALF_DIM = PEER_KEY_DIM // 2
N_KEYS = 128
N_EXPERTS = N_KEYS * N_KEYS
PEER_TOPK_HALF = 16
PEER_TOPK = 16
PEER_CHUNK = 128
N_MOD = 6


def rmsnorm_2(x, g):
    xf = x.astype(jnp.float32)
    y = xf * lax.rsqrt(jnp.mean(xf * xf, axis=-1, keepdims=True) + EPS)
    return (y * g.astype(jnp.float32)).astype(x.dtype)

def layernorm(x, g, b):
    xf = x.astype(jnp.float32)
    mu = jnp.mean(xf, axis=-1, keepdims=True)
    var = jnp.mean(jnp.square(xf - mu), axis=-1, keepdims=True)
    y = (xf - mu) * lax.rsqrt(var + EPS)
    return (y * g.astype(jnp.float32) + b.astype(jnp.float32)).astype(x.dtype)

def causal_window_mean(xg, w):
    s = xg.shape[1]
    xf = xg.astype(jnp.float32)
    cs = jnp.cumsum(xf, axis=1)
    shifted = jnp.pad(cs, ((0, 0), (w, 0), (0, 0)))[:, :s]
    count = jnp.minimum(jnp.arange(1, s + 1), w).astype(jnp.float32)[None, :, None]
    return ((cs - shifted) / count).astype(xg.dtype)

def pool_branch(p, pool_w, pool_scale, pool_up):
    b, s, _ = p.shape
    pooled = jnp.concatenate(
        [causal_window_mean(p[..., i * POOL_GROUP_WIDTH:(i + 1) * POOL_GROUP_WIDTH], w)
         for i, w in enumerate(POOL_WINDOWS)], axis=-1)
    mixed = (pooled - p).reshape(b, s, POOL_GROUPS, POOL_GROUP_WIDTH)
    mixed = jnp.einsum('bsgc,gcd->bsgd', mixed, pool_w).reshape(b, s, POOL_WIDTH)
    return (mixed * pool_scale) @ pool_up

def conformer_branch(a, dw_kernel, dw_bias, ln_g, ln_b, conv_out):
    glu = a[..., :CONV_WIDTH] * jax.nn.sigmoid(a[..., CONV_WIDTH:])
    y = lax.conv_general_dilated(
        glu, dw_kernel[:, None, :].astype(glu.dtype), window_strides=(1,),
        padding=[(CONV_KERNEL - 1, 0)], dimension_numbers=('NWC', 'WIO', 'NWC'),
        feature_group_count=CONV_WIDTH) + dw_bias
    y = layernorm(y, ln_g, ln_b)
    y = y * jax.nn.sigmoid(y)
    return y @ conv_out

def peer(h, w_query, keys_1, keys_2, expert_u, expert_v):
    b, s, d = h.shape
    flat = h.reshape(b * s // PEER_CHUNK, PEER_CHUNK, d)

    def chunk_fn(hc):
        q = (hc @ w_query).reshape(PEER_CHUNK, PEER_HEADS, PEER_KEY_DIM)
        s1 = jnp.einsum('chk,nk->chn', q[..., :PEER_HALF_DIM], keys_1)
        s2 = jnp.einsum('chk,nk->chn', q[..., PEER_HALF_DIM:], keys_2)
        v1, i1 = lax.top_k(s1, PEER_TOPK_HALF)
        v2, i2 = lax.top_k(s2, PEER_TOPK_HALF)
        cand = (v1[..., :, None] + v2[..., None, :]).reshape(PEER_CHUNK, PEER_HEADS, -1)
        cand_idx = (i1[..., :, None] * N_KEYS + i2[..., None, :]).reshape(PEER_CHUNK, PEER_HEADS, -1)
        top_s, pos = lax.top_k(cand, PEER_TOPK)
        experts = jnp.take_along_axis(cand_idx, pos, axis=-1)
        gate = jax.nn.softmax(top_s.astype(jnp.float32), axis=-1).astype(hc.dtype)
        u = jnp.take(expert_u, experts, axis=0)
        act = jax.nn.gelu(jnp.einsum('chkd,cd->chk', u, hc))
        v = jnp.take(expert_v, experts, axis=0)
        return jnp.einsum('chk,chkd->cd', gate * act, v)

    return lax.map(chunk_fn, flat).reshape(b, s, d)

def second_inputs(seed: int = 0) -> dict:
    key = jax.random.key(seed)
    ks = jax.random.split(key, 24)

    def nrm(k, shape, scale):
        return jax.random.normal(k, shape, jnp.float32) * scale

    def gain(k, shape):
        return 1.0 + 0.05 * jax.random.normal(k, shape, jnp.float32)

    L = DEPTH_2
    return {
        "x": nrm(ks[0], (BATCH, SEQ, D_MODEL), 1.0),
        "c": nrm(ks[1], (BATCH, D_MODEL), 1.0),
        "ada_w": nrm(ks[2], (L, D_MODEL, N_MOD * D_MODEL), 0.5 * D_MODEL ** -0.5),
        "ada_b": nrm(ks[3], (L, N_MOD * D_MODEL), 0.01),
        "norm1_g": gain(ks[4], (L, D_MODEL)),
        "w_in": nrm(ks[5], (L, D_MODEL, IN_WIDTH), D_MODEL ** -0.5),
        "b_in": nrm(ks[6], (L, IN_WIDTH), 0.01),
        "pool_w": nrm(ks[7], (L, POOL_GROUPS, POOL_GROUP_WIDTH, POOL_GROUP_WIDTH), POOL_GROUP_WIDTH ** -0.5),
        "pool_scale": gain(ks[8], (L, POOL_WIDTH)),
        "pool_up": nrm(ks[9], (L, POOL_WIDTH, D_MODEL), POOL_WIDTH ** -0.5),
        "dw_kernel": nrm(ks[10], (L, CONV_KERNEL, CONV_WIDTH), CONV_KERNEL ** -0.5),
        "dw_bias": nrm(ks[11], (L, CONV_WIDTH), 0.01),
        "conv_ln_g": gain(ks[12], (L, CONV_WIDTH)),
        "conv_ln_b": nrm(ks[13], (L, CONV_WIDTH), 0.01),
        "conv_out": nrm(ks[14], (L, CONV_WIDTH, D_MODEL), CONV_WIDTH ** -0.5),
        "w_out": nrm(ks[15], (L, D_MODEL, D_MODEL), D_MODEL ** -0.5),
        "norm2_g": gain(ks[16], (L, D_MODEL)),
        "w_query": nrm(ks[17], (L, D_MODEL, PEER_HEADS * PEER_KEY_DIM), D_MODEL ** -0.5),
        "sub_keys_1": nrm(ks[18], (L, N_KEYS, PEER_HALF_DIM), PEER_HALF_DIM ** -0.5),
        "sub_keys_2": nrm(ks[19], (L, N_KEYS, PEER_HALF_DIM), PEER_HALF_DIM ** -0.5),
        "expert_u": nrm(ks[20], (L, N_EXPERTS, D_MODEL), D_MODEL ** -0.5),
        "expert_v": nrm(ks[21], (L, N_EXPERTS, D_MODEL), PEER_HEADS ** -0.5),
        "final_g": gain(ks[22], (D_MODEL,)),
    }

def second_block(x, c, ada_w, ada_b, norm1_g, w_in, b_in, pool_w, pool_scale, pool_up,
              dw_kernel, dw_bias, conv_ln_g, conv_ln_b, conv_out, w_out, norm2_g,
              w_query, sub_keys_1, sub_keys_2, expert_u, expert_v, final_g):
    c_act = jax.nn.silu(c)
    for l in range(DEPTH_2):
        mod = c_act @ ada_w[l] + ada_b[l]
        shift1, scale1, gate1, shift2, scale2, gate2 = [
            m[:, None, :] for m in jnp.split(mod, N_MOD, axis=-1)]

        h = rmsnorm_2(x, norm1_g[l]) * (1.0 + scale1) + shift1
        proj = h @ w_in[l] + b_in[l]
        p = proj[..., :POOL_WIDTH]
        a = proj[..., POOL_WIDTH:POOL_WIDTH + 2 * CONV_WIDTH]
        g = proj[..., POOL_WIDTH + 2 * CONV_WIDTH:]
        y_pool = pool_branch(p, pool_w[l], pool_scale[l], pool_up[l])
        y_conv = conformer_branch(a, dw_kernel[l], dw_bias[l], conv_ln_g[l], conv_ln_b[l], conv_out[l])
        merged = jax.nn.sigmoid(g[..., :D_MODEL]) * y_pool + jax.nn.sigmoid(g[..., D_MODEL:]) * y_conv
        x = x + gate1 * (merged @ w_out[l])

        h2 = rmsnorm_2(x, norm2_g[l]) * (1.0 + scale2) + shift2
        x = x + gate2 * peer(h2, w_query[l], sub_keys_1[l], sub_keys_2[l], expert_u[l], expert_v[l])
    return rmsnorm_2(x, final_g)


def setup_inputs(seed=0):
    out = dict(first_inputs(seed))
    for name, value in second_inputs(seed + 1).items():
        if name != "x":
            out[name + "_2"] = value
    return out


def reference(
    x, c, positions, ada_w, ada_b, norm_mix, norm_ffn, gla_w_in, gla_w_gate, gla_b_gate,
    gla_g_out, gla_w_out, mla_w_in, mla_g_q, mla_w_q_up, mla_g_kv, mla_w_kv_up, mla_w_out,
    ffn_w_in, ffn_w_out, final_norm, c_2, ada_w_2, ada_b_2, norm1_g_2, w_in_2, b_in_2, pool_w_2,
    pool_scale_2, pool_up_2, dw_kernel_2, dw_bias_2, conv_ln_g_2, conv_ln_b_2, conv_out_2,
    w_out_2, norm2_g_2, w_query_2, sub_keys_1_2, sub_keys_2_2, expert_u_2, expert_v_2,
    final_g_2,
):
    x = first_block(
        x, c, positions, ada_w, ada_b, norm_mix, norm_ffn, gla_w_in, gla_w_gate, gla_b_gate,
        gla_g_out, gla_w_out, mla_w_in, mla_g_q, mla_w_q_up, mla_g_kv, mla_w_kv_up, mla_w_out,
        ffn_w_in, ffn_w_out, final_norm,
    )
    return second_block(
        x, c_2, ada_w_2, ada_b_2, norm1_g_2, w_in_2, b_in_2, pool_w_2, pool_scale_2, pool_up_2,
        dw_kernel_2, dw_bias_2, conv_ln_g_2, conv_ln_b_2, conv_out_2, w_out_2, norm2_g_2,
        w_query_2, sub_keys_1_2, sub_keys_2_2, expert_u_2, expert_v_2, final_g_2,
    )


_drawn_inputs = setup_inputs


def setup_inputs(seed=0):
    import zlib

    import numpy as np

    out = dict(_drawn_inputs(seed))
    spreads = {}
    factors = {'norm_mix': 2.87,
     'norm_ffn': 2.754,
     'gla_g_out': 4.477,
     'mla_g_q': 8.0,
     'mla_g_kv': 8.0,
     'final_norm': 2.723,
     'ada_b_2': 5.742,
     'norm1_g_2': 4.989,
     'b_in_2': 34.98,
     'pool_scale_2': 6.468,
     'dw_bias_2': 64.0,
     'conv_ln_g_2': 46.677,
     'conv_ln_b_2': 64.0,
     'norm2_g_2': 19.119}
    for name, (base, spread) in spreads.items():
        noise = np.random.default_rng([zlib.crc32(name.encode()), seed]).standard_normal(out[name].shape)
        drawn = base * np.exp(spread * noise) if base else spread * noise
        out[name] = __import__('jax').numpy.asarray(drawn.astype(out[name].dtype))
    for name, factor in factors.items():
        out[name] = (out[name] * factor).astype(out[name].dtype)
    return out
```

```python
import numpy as np
import concourse.bass as bass
from concourse import mybir

F32 = mybir.dt.float32
F32R = mybir.dt.float32r
U32 = mybir.dt.uint32
I32 = mybir.dt.int32
ALU = mybir.AluOpType
ACT = mybir.ActivationFunctionType
AX = mybir.AxisListType

P = 128
S = 512
D = 1024
DT = D // P
TT = S // P
EPS = 1e-6
RING = 4

GH, GDK, GDV = 4, 128, 256
GLR = 16
TAU = 16.0
GCH = 128
LEVELS = 7

MH, NOPE, ROPE, MVD = 8, 128, 64, 128
QR, KVR = 384, 256
THETA = 10000.0
FF = 2816
FT = FF // P
FSPLIT = (8, 7, 7)

PW, CW, CK = 512, 512, 31
PAD = CK - 1
PPAD = 16
WINDOWS = (2, 4, 8, 16)
NK, PH, TK = 128, 8, 16
GE = 8
NG = NK // GE
ADA0 = 8
WTOK = 32
U_FIRST, U_GATES = 44, 64
U_LAST = NK - U_FIRST - U_GATES

SEGMENTS = (
    ("gla_qk", 8), ("gla_glr", 1), ("gla_v", 8), ("gla_r", 8), ("gla_out", 8),
    ("ffn0_in", 44), ("ffn0_out", 24),
    ("mla_in", 6), ("mla_q", 6), ("mla_k", 2), ("mla_v", 2), ("mla_out", 8),
    ("ffn1_in", 44), ("ffn1_out", 24),
    ("sec_in", 28), ("pool_up", 4), ("conv_out", 4), ("sec_out", 8),
    ("query", 16), ("expert_u", 128), ("expert_v", 128),
)
TILES = (
    ("gla_q", 4), ("gla_k", 4), ("gla_glr", 1), ("gla_v", 8), ("gla_r", 8), ("gla_out", 8),
    ("ffn0_in", 44), ("ffn0_out", 8),
    ("mla_in", 6), ("mla_qn", 8), ("mla_qr", 4), ("mla_k", 8), ("mla_v", 8), ("mla_out", 8),
    ("ffn1_in", 44), ("ffn1_out", 8),
    ("sec_a1", 4), ("sec_a2", 4), ("sec_p", 4), ("sec_g", 16), ("pool_up", 8), ("conv_out", 8), ("sec_out", 8),
    ("query", 16), ("expert_u", 128), ("expert_v", 128),
)


def starts(parts):
    at, out = 0, {}
    for name, n in parts:
        out[name] = at
        at += n
    out["end"] = at
    return out


M0 = starts(SEGMENTS)
T0 = starts(TILES)

COLS = starts((
    ("ada_b", 144), ("norm_mix0", 8), ("norm_mix1", 8), ("norm_ffn0", 8), ("norm_ffn1", 8), ("final_norm", 8),
    ("norm1", 8), ("norm2", 8), ("final_g", 8), ("gla_b_gate", 4), ("gla_g_out", 2), ("mla_g_q", 3), ("mla_g_kv", 2),
    ("b_in", 28), ("pool_scale", 4), ("dw_bias", 4), ("ln_g", 4), ("ln_b", 4), ("dw_kernel", 4 * CK),
))
CONST = starts((("ident", 128), ("ones", 128), ("iota", 128), ("causal_t", 128), ("freq", 1), ("sign", 1),
                ("invcnt", 4 * PPAD)))
NEG = -1e30


def make_consts():
    c = np.zeros((P, CONST["end"]), np.float32)

    def put(name, v):
        c[:, CONST[name]:CONST[name] + v.shape[1]] = v

    p = np.arange(P)
    put("ident", np.eye(P))
    put("ones", np.ones((P, P)))
    put("iota", np.broadcast_to(np.arange(P), (P, P)))
    put("causal_t", np.where(p[None, :] <= p[:, None], 0.0, NEG))
    put("freq", (THETA ** (-np.arange(0, ROPE, 2) / ROPE)).astype(np.float32)[p % (ROPE // 2)][:, None])
    put("sign", np.where(p % ROPE < ROPE // 2, -1.0, 1.0)[:, None])
    t = np.arange(PPAD)
    put("invcnt", np.broadcast_to(np.concatenate([1.0 / np.minimum(t + 1, w) for w in WINDOWS]), (P, 4 * PPAD)))
    return c


def make_level_masks():
    j, i = np.arange(GCH)[:, None], np.arange(GCH)[None, :]
    m = np.zeros((P, LEVELS + 1, GCH), np.uint32)
    for l in range(LEVELS):
        s = GCH >> (l + 1)
        m[:, l] = (j // (2 * s) == i // (2 * s)) & (j // s % 2 == 0) & (i // s % 2 == 1)
    m[:, LEVELS] = i == j
    return m


def make_chunk_mask():
    return np.broadcast_to((np.arange(S) % GCH != 0).astype(np.float32), (P, S)).copy()


def two_blocks(nc, A, out, stop=None):
    sems = []

    def sem(name):
        s = nc.alloc_semaphore(name)
        sems.append(s)
        return s

    base = 16512

    def at(name, offset, shape, dt=F32):
        return nc.alloc_sbuf_tensor_at(name, [P] + shape, dt, offset=base + offset)

    K = 1024
    x = at("x", 0, [DT, S])
    h_hi = at("h_hi", 16 * K, [DT, S], F32R)
    h_lo = at("h_lo", 32 * K, [DT, S], F32R)
    raw = at("raw", 48 * K, [RING, 1024])
    w_hi = at("w_hi", 64 * K, [RING, 1024], F32R)
    w_lo = at("w_lo", 80 * K, [RING, 1024], F32R)
    misc = 96 * K
    cols = at("cols", misc, [COLS["end"]])
    misc += 4 * ((COLS["end"] + 7) // 8 * 8)
    mod = at("mod", misc, [144])
    modg = at("modg", misc + 576, [48])
    misc += 768
    consts = at("consts", misc, [CONST["end"]])
    misc += 4 * ((CONST["end"] + 7) // 8 * 8)
    rstd_off = misc
    rstd = at("rstd", misc, [S])
    misc += 2 * K
    ada_off = misc
    ada = at("ada", misc, [2, D])
    misc += 8 * K
    nsq = at("nsq", ada_off, [4, S])
    cvec = at("cvec", misc, [D])
    misc += 4 * K
    keys = at("keys", misc, [2, NK])
    misc += 1 * K
    ada4 = at("ada4", misc, [RING])
    misc += 32
    AR = (misc + 31) // 32 * 32
    arena_bytes = 229344 - base - AR

    def ar(name, offset, shape, dt=F32):
        n = int(np.prod(shape)) * 4
        assert offset + n <= arena_bytes, (name, offset + n, arena_bytes)
        return at(name, AR + offset, shape, dt)

    g_q = ar("g_q", 0, [GH, S])
    g_k = ar("g_k", 8 * K, [GH, S])
    g_v = ar("g_v", 16 * K, [TT, GH * GDV])
    g_r = ar("g_r", 32 * K, [DT, S])
    g_b = ar("g_b", 48 * K, [GH, S])
    g_E = ar("g_E", 56 * K, [2, S])
    g_qs = ar("g_qs", 60 * K, [2, S])
    g_ks = ar("g_ks", 64 * K, [2, S])
    g_ln = ar("g_ln", 56 * K, [GH, S])
    g_eb = ar("g_eb", 56 * K, [GH, S])
    sq = ar("sq", 56 * K, [DT, S])
    ada0 = ar("ada0", 16 * K, [ADA0, D])
    g_min = ar("g_min", 72 * K, [S])
    g_attn = ar("g_attn", 74 * K, [GH, S])
    g_mask = ar("g_mask", 82 * K, [LEVELS + 1, GCH], U32)
    g_cm = ar("g_cm", 86 * K, [S])
    g_glr = ar("g_glr", 88 * K, [S])
    g_wg = ar("g_wg", 90 * K, [GH * GDK])
    g_dec = ar("g_dec", 92 * K, [GH, TT])
    g_bl = ar("g_bl", 92 * K + 64, [GH, TT])
    g_o = ar("g_o", 56 * K, [DT, S])
    g_S = ar("g_S", 82 * K, [GH, GDV])
    g_kT = ar("g_kT", 86 * K, [2, GH, GDK])
    g_rs = ar("g_rs", 48 * K, [GH, S])
    f_hi = ar("f_hi", 0, [FT, S], F32R)
    f_lo = ar("f_lo", 44 * K, [FT, S], F32R)
    f_sg = ar("f_sg", 88 * K, [2, S])
    f_pr = at("f_pr", rstd_off, [S])
    fsq = ar("fsq", 0, [DT, S])
    m_qn = ar("m_qn", 0, [MH, S])
    msq = ar("msq", 0, [DT, S])
    m_qr = ar("m_qr", 16 * K, [MH // 2, S])
    m_kn = ar("m_kn", 24 * K, [MH, S])
    m_v = ar("m_v", 40 * K, [TT, MH * MVD])
    m_kr = ar("m_kr", 56 * K, [S])
    m_cos = ar("m_cos", 58 * K, [S])
    m_sin = ar("m_sin", 60 * K, [S])
    m_c = ar("m_c", 62 * K, [5, S])
    m_kraw = ar("m_kraw", 72 * K, [S])
    m_sw = ar("m_sw", 74 * K, [S])
    m_t = ar("m_t", 76 * K, [S])
    m_rs = ar("m_rs", 78 * K, [2, S])
    m_pos = ar("m_pos", 82 * K, [S], I32)
    m_ang = ar("m_ang", 84 * K, [S])
    m_P = ar("m_P", 62 * K, [2, S])
    m_PT = ar("m_PT", 66 * K, [2, TT, S])
    m_st = ar("m_st", 86 * K, [MH * TT, 4])
    c_hi = at("c_hi", 16 * K, [5, S], F32R)
    c_lo = at("c_lo", 26 * K, [5, S], F32R)
    ssq = ar("ssq", 0, [DT, S])
    s_a1 = ar("s_a1", 0, [4, S])
    s_csq = ar("s_csq", 0, [4, S])
    s_mix = ar("s_mix", 8 * K, [4, S])
    s_gl = ar("s_gl", 16 * K, [4, PAD + S])
    s_p = ar("s_p", 25 * K, [4, PPAD + S])
    s_pb = ar("s_pb", 34 * K, [2, PPAD + S])
    s_acc = ar("s_acc", 39 * K, [4, S])
    s_sig = ar("s_sig", 47 * K, [S])
    s_sg = ar("s_sg", 49 * K, [16, S])
    s_m2 = ar("s_m2", 81 * K, [S])
    s_pw = ar("s_pw", 83 * K, [4, P])
    s_tmp = ar("s_tmp", 85 * K, [2, S])
    pm_hi = at("pm_hi", 16 * K, [4, S], F32R)
    pm_lo = at("pm_lo", 24 * K, [4, S], F32R)
    cy_hi = at("cy_hi", 32 * K, [4, S], F32R)
    cy_lo = at("cy_lo", 40 * K, [4, S], F32R)
    mg_hi = ar("mg_hi", 0, [DT, S], F32R)
    mg_lo = ar("mg_lo", 16 * K, [DT, S], F32R)
    psq = ar("psq", 32 * K, [DT, S])
    r_q = ar("r_q", 0, [2 * PH, S])
    w_st = ar("w_st", 0, [2, NK, WTOK])
    r_s = ar("r_s", 32 * K, [TT, 2 * PH, NK])
    oh_ahi = ar("oh_ahi", 32 * K, [8, NK], F32R)
    oh_alo = ar("oh_alo", 36 * K, [8, NK], F32R)
    oh_b = ar("oh_b", 40 * K, [8, NK], F32R)
    r_w = ar("r_w", 64 * K, [2 * PH, NK])
    r_oh = ar("r_oh", 64 * K, [PH, TK, TK])
    r_cand = ar("r_cand", 72 * K, [PH, TK * TK])
    r_wait = at("r_wait", rstd_off, [1])
    r_v = ar("r_v", 80 * K, [2 * PH, TK])
    r_ix = ar("r_ix", 81 * K, [2 * PH, TK], U32)
    r_ixf = ar("r_ixf", 82 * K, [2 * PH, TK])
    r_top = ar("r_top", 83 * K, [PH, TK])
    r_pos = ar("r_pos", 83 * K + 512, [PH, TK], U32)
    r_k = ar("r_k", 84 * K, [2, PH, TK], U32)
    r_kf = ar("r_kf", 85 * K, [2, PH, TK])
    r_i = ar("r_i", 86 * K, [3, TT, P])
    r_z = ar("r_z", 92 * K, [2, TT, PH])
    g_act = at("g_act", ada_off, [2, S])
    r_T = at("r_T", ada_off + 4 * K, [4, S])
    wa_hi = ar("wa_hi", 0, [2, GE, S], F32R)
    wa_lo = ar("wa_lo", 32 * K, [2, GE, S], F32R)
    e_w = ar("e_w", 64 * K, [S // WTOK, GE, WTOK])
    e_g = ar("e_g", 80 * K, [4, S])
    e_t = ar("e_t", 88 * K, [S])
    osq = ar("osq", 64 * K, [DT, S])

    ps = nc.alloc_psum_tensor("ps", [P, RING, 512], F32)
    pa = nc.alloc_psum_tensor("pa", [P, 4, 512], F32)
    gates_dram = nc.dram_tensor("gate_matrix", [S // WTOK, P, NK, WTOK], F32, kind="Internal").ap()
    act_dram = nc.dram_tensor("expert_act", [NK, P, S], F32, kind="Internal").ap()

    def col(name, i, rows=P):
        return cols[0:rows, COLS[name] + i:COLS[name] + i + 1]

    def const(name, n, rows=P):
        return consts[0:rows, CONST[name]:CONST[name] + n]

    ident, ones = const("ident", P), const("ones", P)
    iota = const("iota", P)

    def bc(ap, axis, n):
        a = ap.unsqueeze(axis)
        shape = list(a.shape)
        shape[axis] = n
        return a.to_broadcast(shape)

    ld_x, ld_c, ld_m = sem("ld_x"), sem("ld_c"), sem("ld_m")
    ld_v = [sem(f"ld_v{i}") for i in range(3)]
    raw_in = [sem(f"raw_in{i}") for i in range(RING)]
    ada_in = [sem(f"ada_in{i}") for i in range(2)]
    ada0_in = [sem(f"ada0_in{i}") for i in range(ADA0)]
    hi_done, lo_done = sem("hi_done"), sem("lo_done")
    blk_done = sem("blk_done")
    tile_free = sem("tile_free")
    ada_done, mod_done, cvec_done = sem("ada_done"), sem("mod_done"), sem("cvec_done")
    sq_ready, acc_done, ss_done, rs_ready = (sem(n) for n in ("sq_ready", "acc_done", "ss_done", "rs_ready"))
    t_ready, hh_ready, h_ready, fin_ready = (sem(n) for n in ("t_ready", "hh_ready", "h_ready", "fin_ready"))
    dve_own, act_own = sem("dve_own"), sem("act_own")
    z_done, abs_done, ln_done, scan_done = (sem(n) for n in ("z_done", "abs_done", "ln_done", "scan_done"))
    lv_d, lv_e, lv_q, lv_mm, lv_cp = (sem(n) for n in ("lv_d", "lv_e", "lv_q", "lv_mm", "lv_cp"))
    dec_d, dec_e, qe_ready = sem("dec_d"), sem("dec_e"), sem("qe_ready")
    oq_ready, oss_done, ors_ready, og_ready, ot_ready, oh_hi, o_ready = (
        sem(n) for n in ("oq_ready", "oss_done", "ors_ready", "og_ready", "ot_ready", "oh_hi", "o_ready"))
    kt_mm, kt_out, st_mm, st_out, o_mm, o_out, r_silu = (sem(n) for n in ("kt_mm", "kt_out", "st_mm", "st_out", "o_mm", "o_out", "r_silu"))
    sil_done, fh_ready, f_ready, ada_out = (sem(n) for n in ("sil_done", "fh_ready", "f_ready", "ada_out"))
    ang_done, trig_done = sem("ang_done"), sem("trig_done")
    c_sq, c_ss, c_rs, c_t, c_h, c_rd = (sem(n) for n in ("c_sq", "c_ss", "c_rs", "c_t", "c_h", "c_rd"))
    k_raw, sw_done, qr_done, kr_done = sem("k_raw"), sem("sw_done"), sem("qr_done"), sem("kr_done")
    at_s, at_m, at_p, at_n, at_T, at_To, at_o, at_oh, at_ol = (sem(n) for n in ("at_s", "at_m", "at_p", "at_n", "at_T", "at_To", "at_o", "at_oh", "at_ol"))
    glu_done, conv_done, cmu, cx, csq, cvar, crs, ct, cyh, cyl = (
        sem(n) for n in ("glu_done", "conv_done", "cmu", "cx", "csq", "cvar", "crs", "ct", "cyh", "cyl"))
    mix_done, pw_mm, pw_out, pmh, pml, mgh, mgt, mg_done = (
        sem(n) for n in ("mix_done", "pw_mm", "pw_out", "pmh", "pml", "mgh", "mgt", "mg_done"))
    rs_mm, rs_out, top_done, gx_done, gate_done, rt_mm, rt_done = (
        sem(n) for n in ("rs_mm", "rs_out", "top_done", "gx_done", "gate_done", "rt_mm", "rt_done"))
    oh_ready, wb_mm, wb_free = (sem(n) for n in ("oh_ready", "wb_mm", "wb_free"))
    act_st = [sem(f"act_st{i}") for i in range(2)]
    w_out_st = [sem(f"w_out_st{i}") for i in range(2)]
    e_w_in = sem("e_w_in")
    e_g_in = [sem(f"e_g_in{i}") for i in range(4)]
    wa_t, wa_h, wa_done = sem("wa_t"), sem("wa_h"), sem("wa_done")
    y_ready, st_out_done = sem("y_ready"), sem("st_out_done")
    assert len(sems) < 200

    class Own:

        def __init__(self, s):
            self.s, self.n, self.loop = s, 0, None

        def link(self, eng, ins):
            ins.then_inc(self.s, 1)
            if self.loop is None:
                self.n += 1
                eng.wait_ge(self.s, self.n)
            else:
                i, per, k = self.loop
                self.loop = (i, per, k + 1)
                eng.wait_ge(self.s, i * per + (self.n + k + 1))

        def begin(self, i, per):
            self.loop = (i, per, 0)

        def end(self, times):
            _, per, k = self.loop
            assert k == per, (k, per)
            self.n, self.loop = self.n + per * times, None

    X_TILE = {1: T0["gla_out"], 2: T0["ffn0_out"], 3: T0["mla_out"], 4: T0["ffn1_out"], 6: T0["sec_out"],
              7: T0["end"] - DT}
    NORM_BUF = {0: sq, 1: fsq, 2: msq, 3: fsq, 4: ssq, 5: ssq, 6: psq, 7: osq}
    H_USE = {0: 0, 1: 1, 2: 2, 3: 3, 5: 4, 6: 5}
    MODG = {0: 0, 1: 8, 2: 16, 3: 24, 5: 32, 6: 40}
    SHIFT = {0: 0, 1: 24, 2: 48, 3: 72, 5: 96, 6: 120}
    GATE = {0: 16, 1: 40, 2: 64, 3: 88, 5: 112, 6: 136}
    H_FREE = {0: 0, 1: M0["ffn0_in"], 2: M0["mla_in"], 3: M0["ffn1_in"], 5: M0["sec_in"], 6: M0["query"]}
    PLAIN = {4: "final_norm", 7: "final_g"}

    def sp_ada0(sp, j):
        if j >= ADA0:
            sp.wait_ge(ada_done, j - (ADA0 - 1))
        sp.dma_start(ada0[:, j % ADA0, :], A["ada"][j, :, :]).then_inc(ada0_in[j % ADA0], 16)

    def sp_ada(sp, j, slot):
        if not isinstance(j, int) or j >= 50:
            sp.wait_ge(ada_done, j - 1)
        sp.dma_start(ada[:, slot, :], A["ada"][j, :, :]).then_inc(ada_in[slot], 16)

    def sp_raw(sp, m, source, columns):
        n, k = m if isinstance(m, tuple) else (m, m % RING)
        if not isinstance(n, int) or n >= RING:
            sp.wait_ge(lo_done, n - (RING - 1))
        sp.dma_start(raw[:, k, 0:columns], source).then_inc(raw_in[k], 16)

    def sp_segment(sp, name, source, columns):
        m, n = M0[name], dict(SEGMENTS)[name]
        whole = n // RING
        if whole > 1:
            with sp.Fori(0, whole) as i:
                for k in range(RING):
                    sp_raw(sp, (i * RING + (m + k), (m + k) % RING), source[i * RING + k, :, :], columns)
        else:
            whole = 0
        for k in range(whole * RING, n):
            sp_raw(sp, m + k, source[k, :, :], columns)

    def sp_ffn(sp, l):
        j0, m, source = 48 * (l + 1), M0[f"ffn{l}_in"], A[f"ffn{l}_in"]
        for k in range(8):
            sp_raw(sp, m + k, source[k, :, :], 1024)
        sp.wait_ge(ss_done, 2 * l + 2)
        with sp.Fori(2, 2 * FT // RING) as i:
            for k in range(RING):
                sp_raw(sp, (i * RING + (m + k), (m + k) % RING), source[i * RING + k, :, :], 1024)
                sp_ada(sp, i * RING + (j0 + k - 8), k % 2)
        m = M0[f"ffn{l}_out"]

        def out_blocks(i, beside):
            for k in range(12):
                u = 1024 * (k % 3 > 0) + 896 * (k % 3 > 1)
                n = FSPLIT[k % 3] * P
                sp_raw(sp, (i * 12 + (m + k), (m + k) % RING), A[f"ffn{l}_out"][i * 4 + k // 3, :, u:u + n], n)
                if beside and k < 5:
                    for j in range(12 * k // 5, 12 * (k + 1) // 5):
                        sp_ada(sp, j0 + 2 * FT - 8 + j, j % 2)

        out_blocks(0, True)
        out_blocks(1, False)

    def sp_program(sp):
        sp.dma_start(x[:, :, :], A["x"].rearrange("k p t -> p k t")).then_inc(ld_x, 16)
        for j in range(16):
            if j in (11, 13):
                sp_raw(sp, j // 13, A["gla_qk"][j // 13, :, :], 1024)
            sp_ada0(sp, j)
        for m in range(2, RING):
            sp_raw(sp, m, A["gla_qk"][m, :, :], 1024)
        for m in range(RING, 8):
            sp_raw(sp, m, A["gla_qk"][m, :, :], 1024)
        for j in range(16, 24):
            sp_ada0(sp, j)
        sp_raw(sp, M0["gla_glr"], A["gla_glr"][:, :], 1024)
        for m in range(8):
            if m < 6:
                for j in range(24 + 4 * m, 28 + 4 * m):
                    sp_ada0(sp, j)
            sp_raw(sp, M0["gla_v"] + m, A["gla_v"][m, :, :], 1024)
        for name in ("gla_r", "gla_out"):
            sp_segment(sp, name, A[name], 1024)
        if stop == "gla":
            return
        sp_ffn(sp, 0)
        if stop == "ffn0":
            for k in range(3):
                sp_raw(sp, M0["mla_in"] + k, A["mla_in"][k, :, :], 1024)
            return
        sp_segment(sp, "mla_in", A["mla_in"], 1024)
        sp_segment(sp, "mla_q", A["mla_q"], 6 * P)
        sp_segment(sp, "mla_k", A["mla_k"], 1024)
        sp_segment(sp, "mla_v", A["mla_v"], 1024)
        sp_segment(sp, "mla_out", A["mla_out"], 1024)
        if stop == "mla":
            return
        sp_ffn(sp, 1)
        if stop == "ffn1":
            for k in range(3):
                sp_raw(sp, M0["sec_in"] + k, A["sec_in"][k, :, :], 1024)
            return
        for name in ("sec_in", "pool_up", "conv_out", "sec_out"):
            sp_segment(sp, name, A[name], 1024)
        if stop == "sec":
            return
        sp_segment(sp, "query", A["query"], 1024)
        mu = M0["expert_u"]
        with sp.Fori(0, (NK - 12) // RING) as i:
            for k in range(RING):
                sp_raw(sp, (i * RING + (mu + k), (mu + k) % RING), A["expert_u"][i * RING + k, :, :], 1024)
        mv = M0["expert_v"]

        def group_in(g, k):
            if not isinstance(g, int) or k >= 4:
                sp.wait_ge(wa_t, g * GE + (k - 3))
            sp.dma_start(e_g[:, k % 4, :], act_dram[g * GE + k, :, :]).then_inc(e_g_in[k % 4], 16)

        def gates_in(g):
            if not isinstance(g, int):
                sp.wait_ge(wa_t, g * GE)
            sp.dma_start(e_w[:, :, :, :], gates_dram[:, :, bass.ts(g, GE), :].rearrange("t p e k -> p t e k"))\
              .then_inc(e_w_in, 16)

        for k in range(2):
            sp.wait_ge(w_out_st[k], 16 * (S // WTOK) // 2)
            sp.wait_ge(act_st[k], 16 * GE // 2)
        sp.wait_ge(rt_mm, 1)
        gates_in(0)
        for k in range(4):
            group_in(0, k)
        for k in range(12):
            sp_raw(sp, mu + NK - 12 + k, A["expert_u"][NK - 12 + k, :, :], 1024)
        for k in range(4, GE):
            group_in(0, k)
        for k in range(3):
            sp_raw(sp, mv + k, A["expert_v"][k, :, :], 1024)
        for k in range(2):
            sp.wait_ge(act_st[k], 16 * NK // 2)
        with sp.Fori(0, NG - 1) as g:
            for k in range(GE):
                sp_raw(sp, (g * GE + (mv + k + 3), (mv + k + 3) % RING), A["expert_v"][g * GE + (k + 3), :, :], 1024)
                if k == 0:
                    gates_in(g + 1)
                group_in(g + 1, k)
        for k in range(3, GE):
            m = (NG - 1) * GE + k
            sp_raw(sp, mv + m, A["expert_v"][m, :, :], 1024)

    def pool_program(pool):
        last = HI_END

        def split(m, k):
            pool.wait_ge(hi_done, m + 1)
            nc.gpsimd.tensor_tensor(w_lo[:, k, :], raw[:, k, :], w_hi[:, k, :].bitcast(F32), ALU.subtract)\
              .then_inc(lo_done, 1)

        with pool.Fori(0, last // RING) as i:
            for k in range(RING):
                split(i * RING + k, k)
        for m in range(last // RING * RING, last):
            split(m, m % RING)

    own_a, own_d = Own(act_own), Own(dve_own)

    def act_hi(act, m, k, i=None, per=0):
        act.wait_ge(raw_in[k], 16 * (m // RING + 1) if i is None else i * (16 * (per // RING)) + 16 * (m // RING + 1))
        if m >= RING:
            act.wait_ge(blk_done, m - (RING - 1) if i is None else i * per + (m - (RING - 1)))
        nc.scalar.activation(w_hi[:, k, :], raw[:, k, :], ACT.Copy).then_inc(hi_done, 1)

    class Hi:

        def __init__(self, act):
            self.act, self.next = act, 0

        def upto(self, m):
            while self.next <= min(m, HI_END - 1):
                act_hi(self.act, self.next, self.next % RING)
                self.next += 1

        def loop(self, i, per, m):
            act_hi(self.act, m + 3, (m + 3) % RING, i, per)

        def skip(self, n):
            self.next += n

    HI_END = M0["end"] if stop is None else {"gla": M0["ffn0_in"], "ffn0": M0["mla_in"] + 3, "mla": M0["ffn1_in"],
                                             "ffn1": M0["sec_in"] + 3, "sec": M0["query"]}[stop]

    def act_norm(act, n, hi=None, out=None):
        buf = NORM_BUF[n]
        if n == 7:
            for b in range(2):
                act.wait_ge(act_st[b], 16 * NK // 2)
        for k in range(DT):
            if out:
                hi.upto(M0[out[0]] + out[1] * (k + 1) + 2)
            if n in (2, 4) and k == 0:
                act.wait_ge(ada_done, 48 * (n // 2 + 1))
            if n == 5:
                act.wait_ge(fin_ready, k + 1)
            elif n:
                act.wait_ge(tile_free, X_TILE[n] + k + 1)
            elif k == 0:
                act.wait_ge(ld_x, 16)
            if k >= 4:
                act.wait_ge(acc_done, 6 * n + max(1, k - 4))
            nc.scalar.activation(nsq[:, k % 4, :], x[:, k, :], ACT.Square).then_inc(sq_ready, 1)
        act.wait_ge(ss_done, n + 1)
        own_a.link(act, nc.scalar.activation(rstd[:, :], pa[:, 0, :], ACT.Ln, scale=1.0 / D, bias=EPS))
        nc.scalar.activation(rstd[:, :], rstd[:, :], ACT.Exp, scale=-0.5).then_inc(rs_ready, 1)
        if n in PLAIN:
            return
        if n == 0:
            hi.upto(1)
        u = H_USE[n]
        if H_FREE[n]:
            act.wait_ge(blk_done, H_FREE[n])
        act.wait_ge(mod_done, MOD_STAGE[n])
        for k in range(DT):
            act.wait_ge(t_ready, DT * u + k + 1)
            nc.scalar.activation(h_hi[:, k, :], buf[:, k, :], ACT.Identity,
                                 bias=mod[:, SHIFT[n] + k:SHIFT[n] + k + 1]).then_inc(hh_ready, 1)

    MOD_STAGE = {0: 1, 1: 2, 2: 3, 3: 3, 5: 4, 6: 4}
    ITEMS = GH * (LEVELS + 1)

    def item_level(n):
        h, l = divmod(n, LEVELS + 1)
        return h, l, h * LEVELS + min(l, LEVELS)

    def items_by(b):
        return 0 if b < 3 else min(ITEMS, (b - 2) * 3)

    R_ITEMS, R_CHUNKS = 4, 6

    def act_gla(act, hi):
        for t in range(2 * GH):
            hi.upto(t + 3)
            act.wait_ge(blk_done, t + 1)
            dst = g_q[:, t, :] if t < GH else g_k[:, t - GH, :]
            nc.scalar.activation(dst, ps[:, t % RING, :], ACT.Copy, scale=GDK ** -0.5 if t < GH else 1.0)\
              .then_inc(tile_free, 1)
        m = M0["gla_glr"]
        hi.upto(m + 3)
        act.wait_ge(blk_done, m + 1)
        nc.scalar.activation(g_glr[0:GLR, :], ps[0:GLR, T0["gla_glr"] % RING, :], ACT.Copy).then_inc(tile_free, 1)
        act.wait_ge(h_ready, DT)
        for t in range(GH):
            act.wait_ge(z_done, t + 1)
            nc.scalar.activation(g_ln[:, t, :], pa[:, t, :], ACT.Abs, bias=col("gla_b_gate", t)).then_inc(abs_done, 1)
            act.wait_ge(abs_done, t + 1)
            own_a.link(act, nc.scalar.activation(g_ln[:, t, :], g_ln[:, t, :], ACT.Exp, scale=-1.0))
            nc.scalar.activation(g_ln[:, t, :], g_ln[:, t, :], ACT.Ln, bias=1.0).then_inc(ln_done, 1)

        taken = [0]

        def levels(n):
            while taken[0] < min(n, ITEMS):
                h, l, e = item_level(taken[0])
                if l < LEVELS:
                    act.wait_ge(lv_d, e + 1)
                    own_a.link(act, nc.scalar.activation(g_E[:, e % 2, :], g_E[:, e % 2, :], ACT.Abs))
                    nc.scalar.activation(g_E[:, e % 2, :], g_E[:, e % 2, :], ACT.Exp, scale=-1.0 / TAU).then_inc(lv_e, 1)
                taken[0] += 1

        for b in range(8 + R_ITEMS):
            m, T = M0["gla_v"] + b, T0["gla_v"] + b
            hi.upto(m + 3)
            levels(items_by(b) + 1)
            if b == 3:
                act.wait_ge(ada_done, 48)
            if b in (3, 7):
                act.wait_ge(blk_done, m + 1)
                c = b // 4
                for t in range(TT):
                    nc.scalar.activation(g_v[:, t, 512 * c:512 * (c + 1)], ps[:, (T - 3 + t) % RING, :], ACT.Copy)\
                      .then_inc(tile_free, 1)
            elif b >= 8:
                act.wait_ge(blk_done, m + 1)
                nc.scalar.activation(g_r[:, b - 8, :], ps[:, T % RING, :], ACT.Copy).then_inc(tile_free, 1)
        levels(ITEMS)
        act.wait_ge(lv_cp, ITEMS)
        nc.scalar.activation(g_eb[:, :, :], g_b[:, :, :], ACT.Exp, scale=1.0 / TAU).then_inc(dec_e, 1)
        act.wait_ge(dec_d, 1)
        nc.scalar.activation(g_dec[:, :, :], g_bl[:, :, :], ACT.Exp, scale=1.0 / TAU).then_inc(dec_e, 1)
        act.wait_ge(dec_d, 2)
        nc.scalar.activation(g_b[:, :, :], g_b[:, :, :], ACT.Exp, scale=1.0 / TAU).then_inc(dec_e, 1)
        for k in range(R_ITEMS, R_CHUNKS):
            hi.upto(M0["gla_r"] + k + 3)
            act.wait_ge(blk_done, M0["gla_r"] + k + 1)
            nc.scalar.activation(g_r[:, k, :], ps[:, (T0["gla_r"] + k) % RING, :], ACT.Copy).then_inc(tile_free, 1)
        act.wait_ge(tile_free, T0["gla_r"] + R_CHUNKS)
        nc.scalar.activation(g_r[:, 0:R_CHUNKS, :], g_r[:, 0:R_CHUNKS, :], ACT.Silu).then_inc(r_silu, 1)
        act.wait_ge(qe_ready, 2)
        for c in range(TT):
            if c < TT - 1:
                act.wait_ge(kt_mm, c + 1)
                if c >= 2:
                    act.wait_ge(st_mm, c - 1)
                nc.scalar.activation(g_kT[:, c % 2, :, :], ps[:, 2 + c % 2, :].rearrange("p (h k) -> p h k", h=GH), ACT.Copy)\
                  .then_inc(kt_out, 1)
            act.wait_ge(o_mm, c + 1)
            for a in range(2):
                nc.scalar.activation(g_o[:, a::2, c * GCH:(c + 1) * GCH],
                                     pa[:, 2 * (c % 2) + a, :].rearrange("p (h t) -> p h t", h=GH), ACT.Copy)\
                  .then_inc(o_out, 1)
        act.wait_ge(o_out, 2 * TT)
        for k in range(DT):
            if k >= 4:
                act.wait_ge(oss_done, k // 2 - 1)
            nc.scalar.activation(nsq[:, k % 4, :], g_o[:, k, :], ACT.Square).then_inc(oq_ready, 1)
        for k in range(R_CHUNKS, DT):
            hi.upto(M0["gla_r"] + k + 2)
        act.wait_ge(oss_done, GH)
        own_a.link(act, nc.scalar.activation(g_rs[:, :, :], pa[:, :, :], ACT.Ln, scale=1.0 / GDV, bias=EPS))
        nc.scalar.activation(g_rs[:, :, :], g_rs[:, :, :], ACT.Exp, scale=-0.5).then_inc(ors_ready, 1)
        for k in range(R_CHUNKS, DT):
            hi.upto(M0["gla_r"] + k + 3)
            act.wait_ge(blk_done, M0["gla_r"] + k + 1)
            nc.scalar.activation(g_r[:, k, :], ps[:, (T0["gla_r"] + k) % RING, :], ACT.Silu).then_inc(tile_free, 1)
        for k in range(DT):
            act.wait_ge(ot_ready, k + 1)
            nc.scalar.activation(h_hi[:, k, :], g_o[:, k, :], ACT.Copy).then_inc(oh_hi, 1)

    def act_ffn(act, hi, l):
        m, T = M0[f"ffn{l}_in"], T0[f"ffn{l}_in"]
        hi.upto(m + 2)
        with act.Fori(0, FT // 2) as i:
            for q in range(2):
                hi.loop(i, 4, m + 2 * q)
                hi.loop(i, 4, m + 2 * q + 1)
                act.wait_ge(blk_done, i * 4 + (m + 2 * q + 1))
                act.wait_ge(tile_free, i * 4 + (T + 2 * q - 2))
                nc.scalar.activation(f_sg[:, q, :], ps[:, (T + 2 * q) % RING, :], ACT.Silu).then_inc(sil_done, 1)
        hi.skip(2 * FT)

    def act_mla(act, hi):
        act.dma_start(m_pos[:, :], A["positions"].partition_broadcast(P)).then_inc(ld_v[2], 16)
        m, T = M0["mla_in"], T0["mla_in"]
        act.wait_ge(h_ready, 3 * DT)
        for t in range(5):
            hi.upto(m + t + 3)
            act.wait_ge(blk_done, m + t + 1)
            nc.scalar.activation(msq[:, t, :], ps[:, (T + t) % RING, :], ACT.Square).then_inc(c_sq, 1)
            nc.scalar.activation(m_c[:, t, :], ps[:, (T + t) % RING, :], ACT.Copy).then_inc(tile_free, 1)
        hi.upto(m + 8)
        act.wait_ge(blk_done, m + 6)
        krope = ps[:, (T + 5) % RING, :]
        nc.scalar.activation(m_kraw[:, :], krope, ACT.Copy)
        for q in range(4):
            nc.scalar.activation(m_sw[32 * q:32 * q + 32, :], krope[32 * (q ^ 1):32 * (q ^ 1) + 32, :], ACT.Copy)\
              .then_inc(k_raw, 1)
        act.wait_ge(k_raw, 4)
        nc.scalar.activation(m_st[:, 0, 0:1], m_kraw[:, 0:1], ACT.Copy).then_inc(tile_free, 1)
        act.wait_ge(ang_done, 1)
        nc.scalar.activation(m_sin[:, :], m_ang[:, :], ACT.Sin, scale=const("sign", 1))
        nc.scalar.activation(m_cos[:, :], m_t[:, :], ACT.Sin).then_inc(trig_done, 1)
        act.wait_ge(c_ss, 1)
        own_a.link(act, nc.scalar.activation(m_rs[:, 0, :], pa[:, 1, :], ACT.Ln, scale=1.0 / QR, bias=EPS))
        own_a.link(act, nc.scalar.activation(m_rs[:, 1, :], pa[:, 2, :], ACT.Ln, scale=1.0 / KVR, bias=EPS))
        nc.scalar.activation(m_rs[:, :, :], m_rs[:, :, :], ACT.Exp, scale=-0.5).then_inc(c_rs, 1)
        for t in range(5):
            act.wait_ge(c_t, t + 1)
            nc.scalar.activation(c_hi[:, t, :], m_c[:, t, :], ACT.Copy).then_inc(c_h, 1)
        T = T0["mla_qn"]
        for t in range(12):
            m = M0["mla_q"] + t // 2
            hi.upto(m + 3)
            act.wait_ge(blk_done, m + 1)
            bank = ps[:, (T + t) % RING, :]
            if t < MH:
                nc.scalar.activation(m_qn[:, t, :], bank, ACT.Copy).then_inc(tile_free, 1)
            else:
                j = t - MH
                act.wait_ge(kr_done, 1)
                if j >= 2:
                    act.wait_ge(qr_done, j - 1)
                dst = (m_sw, m_kraw)[j % 2]
                for q in range(4):
                    nc.scalar.activation(dst[32 * q:32 * q + 32, :], bank[32 * (q ^ 1):32 * (q ^ 1) + 32, :], ACT.Copy)\
                      .then_inc(sw_done, 1)
        T = T0["mla_k"]
        act.wait_ge(tile_free, T)
        for t in range(MH):
            m = M0["mla_k"] + t // 4
            hi.upto(m + 3)
            act.wait_ge(blk_done, m + 1)
            nc.scalar.activation(m_kn[:, t, :], ps[:, (T + t) % RING, :], ACT.Copy).then_inc(tile_free, 1)
        T = T0["mla_v"]
        for c in range(2):
            m = M0["mla_v"] + c
            hi.upto(m + 3)
            act.wait_ge(blk_done, m + 1)
            for t in range(TT):
                nc.scalar.activation(m_v[:, t, 512 * c:512 * (c + 1)], ps[:, (T + 4 * c + t) % RING, :], ACT.Copy)\
                  .then_inc(tile_free, 1)
        hi.upto(M0["mla_out"] + 2)
        act.wait_ge(c_rd, 5)
        act.wait_ge(qr_done, MH // 2)
        n_it = MH * TT
        for s in range(n_it + 3):
            if s < n_it:
                n = P * (s % TT + 1)
                act.wait_ge(at_m, s + 1)
                if s >= 2:
                    act.wait_ge(at_T, s - 1)
                nc.scalar.activation(m_P[:, s % 2, 0:n], pa[:, s % 3, 0:n], ACT.Exp, bias=m_st[:, s, 1:2],
                                     scale=MSCALE, accum_out=m_st[:, s, 2:3]).then_inc(at_p, 1)
            if 2 <= s < n_it + 2:
                h, qb = divmod(s - 2, TT)
                act.wait_ge(at_T, s - 1)
                if h >= 2:
                    act.wait_ge(at_o, h - 1)
                nc.scalar.activation(m_PT[:, h % 2, 0:qb + 1, qb * P:(qb + 1) * P],
                                     ps[:, s % 2, 0:(qb + 1) * P].rearrange("p (k q) -> p k q", q=P), ACT.Copy)\
                  .then_inc(at_To, 1)
            if s >= 6 and (s - 6) % TT == 0:
                h = (s - 6) // TT
                act.wait_ge(at_o, h + 1)
                nc.scalar.activation(h_hi[:, h, :], ps[:, 2 + h % 2, :], ACT.Copy).then_inc(at_oh, 1)

    def act_second(act, hi):
        m, T = M0["sec_in"], T0["sec_a1"]
        act.wait_ge(h_ready, 5 * DT)
        for t in range(28):
            hi.upto(m + t + 3)
            act.wait_ge(blk_done, m + t + 1)
            bank, b = ps[:, (T + t) % RING, :], col("b_in", (4 + t if t < 8 else t - 8 if t < 12 else t))
            if t < 4:
                nc.scalar.activation(s_a1[:, t, :], bank, ACT.Identity, bias=b).then_inc(tile_free, 1)
            elif t < 8:
                if t > 4:
                    act.wait_ge(glu_done, t - 4)
                nc.scalar.activation(s_sig[:, :], bank, ACT.Sigmoid, bias=b).then_inc(tile_free, 1)
            elif t < 12:
                nc.scalar.activation(s_p[:, t - 8, PPAD:], bank, ACT.Identity, bias=b).then_inc(tile_free, 1)
            else:
                nc.scalar.activation(s_sg[:, t - 12, :], bank, ACT.Sigmoid, bias=b).then_inc(tile_free, 1)
        for g in range(4):
            act.wait_ge(pw_mm, g + 1)
            if g >= 2:
                act.wait_ge(pml, g - 1)
            own_a.link(act, nc.scalar.activation(s_tmp[:, g % 2, :], pa[:, 2 + g % 2, :], ACT.Copy,
                                                 scale=col("pool_scale", g)))
            nc.scalar.activation(pm_hi[:, g, :], s_tmp[:, g % 2, :], ACT.Copy).then_inc(pmh, 1)
        for t in range(4):
            act.wait_ge(cx, t + 1)
            nc.scalar.activation(s_csq[:, t, :], s_acc[:, t, :], ACT.Square).then_inc(csq, 1)
        hi.upto(M0["pool_up"] + 6)
        act.wait_ge(cvar, 1)
        own_a.link(act, nc.scalar.activation(rstd[:, :], pa[:, 1, :], ACT.Ln, scale=1.0 / CW, bias=EPS))
        nc.scalar.activation(rstd[:, :], rstd[:, :], ACT.Exp, scale=-0.5).then_inc(crs, 1)
        for t in range(4):
            act.wait_ge(ct, t + 1)
            own_a.link(act, nc.scalar.activation(s_acc[:, t, :], s_acc[:, t, :], ACT.Silu, bias=col("ln_b", t)))
            nc.scalar.activation(cy_hi[:, t, :], s_acc[:, t, :], ACT.Copy).then_inc(cyh, 1)
        hi.upto(M0["conv_out"] + 4)
        for k in range(DT):
            hi.upto(M0["conv_out"] + k // 2 + 4)
            act.wait_ge(mgt, k + 1)
            nc.scalar.activation(mg_hi[:, k, :], s_tmp[:, k % 2, :], ACT.Copy).then_inc(mgh, 1)

    def act_gelu(act, i, per, m, T, k, base_e):
        act.wait_ge(blk_done, i * per + (m + k + 1))
        if not isinstance(i, int) or base_e + k >= 2:
            act.wait_ge(act_st[k % 2], i * (16 * per // 2) + 16 * ((base_e + k) // 2))
        nc.scalar.activation(g_act[:, k % 2, :], ps[:, (T + k) % RING, :], ACT.Gelu_apprx_tanh)\
          .then_inc(tile_free, 1)
        act.wait_ge(tile_free, i * per + (T + k + 1))
        act.dma_start(act_dram[i * per + (base_e + k), :, :], g_act[:, k % 2, :]).then_inc(act_st[k % 2], 16)

    assert U_FIRST % RING == U_GATES % RING == U_LAST % RING == 0
    WPER = 2 * U_GATES // (S // WTOK)

    def act_peer(act, hi):
        m, T = M0["query"], T0["query"]
        act.wait_ge(h_ready, 6 * DT)
        for t in range(2 * PH):
            hi.upto(m + t + 3)
            act.wait_ge(blk_done, m + t + 1)
            nc.scalar.activation(r_q[:, t, :], ps[:, (T + t) % RING, :], ACT.Copy).then_inc(tile_free, 1)
        for t in range(TT):
            for b in range(4):
                act.wait_ge(rs_mm, 4 * t + b + 1)
                nc.scalar.activation(r_s[:, t, 4 * b:4 * b + 4, :],
                                     pa[:, b, :].rearrange("p (a n) -> p a n", a=4), ACT.Copy).then_inc(rs_out, 1)
        m, T = M0["expert_u"], T0["expert_u"]

        def four(i):
            for k in range(RING):
                hi.loop(i, RING, m + k)
                act_gelu(act, i, RING, m, T, k, 0)

        four(0)
        with act.Fori(1, U_FIRST // RING) as i:
            four(i)
        hi.skip(U_FIRST)
        act.wait_ge(top_done, 1)
        nc.scalar.activation(r_i[:, 2, :, :], r_i[:, 2, :, :], ACT.Exp).then_inc(gx_done, 1)
        act.wait_ge(rt_mm, 1)
        for a in range(2):
            nc.scalar.activation(r_T[:, a, :], pa[:, a, :], ACT.Copy).then_inc(rt_done, 1)
        nc.scalar.activation(r_T[:, 2, :].bitcast(F32R), pa[:, 2, :], ACT.Copy).then_inc(rt_done, 1)
        act.wait_ge(rt_done, 4)
        nc.scalar.activation(r_z[:, 0, 0, 0:1], r_z[:, 1, 0, 0:1], ACT.Copy).then_inc(wb_free, 4)
        m, T = m + U_FIRST, T + U_FIRST

        def two_stages(i):
            for k in range(WPER):
                hi.loop(i, WPER, m + k)
                act_gelu(act, i, WPER, m, T, k, U_FIRST)
                b = k // (WPER // 2)
                n = WTOK // 4 // (WPER // 2)
                for q in range(n * (k % (WPER // 2)), n * (k % (WPER // 2)) + n):
                    g = WTOK // 4 * b + q
                    act.wait_ge(wb_mm, i * (2 * WTOK // 4) + (g + 3))
                    if q == 0 and not isinstance(i, int):
                        act.wait_ge(w_out_st[b], i * 16)
                    nc.scalar.activation(w_st[:, b, :, 4 * q:4 * q + 4].rearrange("p n t -> p t n"),
                                         pa[:, q % 4, :].rearrange("p (t n) -> p t n", t=4), ACT.Copy).then_inc(wb_free, 1)
                if k % (WPER // 2) == WPER // 2 - 1:
                    act.wait_ge(wb_free, i * (2 * WTOK // 4) + (4 + WTOK // 4 * (b + 1)))
                    act.dma_start(gates_dram[i * 2 + b, :, :, :], w_st[:, b, :, :]).then_inc(w_out_st[b], 16)

        two_stages(0)
        with act.Fori(1, S // WTOK // 2) as i:
            two_stages(i)
        hi.skip(U_GATES)
        m, T, done = m + U_GATES, T + U_GATES, U_FIRST + U_GATES
        with act.Fori(0, (U_LAST - GE) // RING) as i:
            for k in range(RING):
                hi.loop(i, RING, m + k)
                act_gelu(act, i, RING, m, T, k, done)
        hi.skip(U_LAST - GE)

        def wa_part(g, k, b, i=None):
            act.wait_ge(wa_t, GE * g + k + 1 if i is None else i * (2 * GE) + (GE * g + k + 1))
            nc.scalar.activation(wa_hi[:, b, k, :], e_t[:, :], ACT.Copy).then_inc(wa_h, 1)

        for b in range(2):
            act.wait_ge(w_out_st[b], 16 * (S // WTOK // 2))
        for k in range(GE):
            q = U_LAST - GE + k
            hi.upto(m + q + 3)
            act_gelu(act, 0, RING, m, T, q, done)
            wa_part(0, k, 0)
        m = M0["expert_v"]
        with act.Fori(0, NG // 2 - 1) as i:
            for g in range(2):
                for k in range(GE):
                    hi.loop(i, 2 * GE, m + GE * g + k)
                    wa_part(g + 1, k, (g + 1) % 2, i)
        hi.skip(GE * (NG - 2))
        for k in range(GE):
            hi.upto(m + GE * (NG - 2) + k + 3)
            wa_part(NG - 1, k, 1)
        hi.upto(M0["end"])

    def act_program(act):
        act.dma_start(cvec[:, :], A["c"].partition_broadcast(P)).then_inc(ld_v[0], 16)
        act.dma_start(consts[:, :], A["consts"]).then_inc(ld_c, 16)
        act.dma_start(cols[:, :], A["cols"]).then_inc(ld_c, 16)
        act.wait_ge(ld_v[0], 16)
        nc.scalar.activation(cvec[:, :], cvec[:, :], ACT.Silu).then_inc(cvec_done, 1)
        act.wait_ge(ld_c, 32)
        hi = Hi(act)
        act_norm(act, 0, hi)
        act.dma_start(g_mask[:, :, :], A["masks"].rearrange("p (l i) -> p l i", i=GCH)).then_inc(ld_m, 16)
        act.dma_start(g_cm[:, :], A["chunk_mask"]).then_inc(ld_m, 16)
        act.dma_start(g_wg[0:GLR, :], A["gla_w_gate"]).then_inc(ld_m, 16)
        act.dma_start(keys[:, :, :], A["keys"].rearrange("p (a n) -> p a n", a=2)).then_inc(ld_m, 16)
        act_gla(act, hi)
        if stop == "gla":
            return
        act_norm(act, 1, hi, ("gla_out", 1))
        act_ffn(act, hi, 0)
        if stop == "ffn0":
            return
        act_norm(act, 2, hi, ("ffn0_out", 3))
        act_mla(act, hi)
        if stop == "mla":
            return
        act.wait_ge(ada_done, 96)
        act.dma_start(cvec[:, :], A["c_2"].partition_broadcast(P)).then_inc(ld_v[1], 16)
        act_norm(act, 3, hi, ("mla_out", 1))
        act.wait_ge(ld_v[1], 16)
        nc.scalar.activation(cvec[:, :], cvec[:, :], ACT.Silu).then_inc(cvec_done, 1)
        act_ffn(act, hi, 1)
        if stop == "ffn1":
            return
        act_norm(act, 4, hi, ("ffn1_out", 3))
        act.dma_start(s_pw[:, :, :], A["pool_w"].rearrange("g c d -> c g d")).then_inc(ld_m, 16)
        act_norm(act, 5)
        act_second(act, hi)
        if stop == "sec":
            return
        act_norm(act, 6, hi, ("sec_out", 1))
        act_peer(act, hi)
        act_norm(act, 7)

    def dve_ada(dve, j, slot, dst):
        first = isinstance(j, int) and j < 48
        w = ada0[:, j % ADA0, :] if first else ada[:, slot, :]
        if first:
            dve.wait_ge(ada0_in[j % ADA0], 16 * (j // ADA0 + 1))
        elif isinstance(j, int):
            dve.wait_ge(ada_in[slot], 16 * ((j - 48) // 2 + 1))
        else:
            i, j, per = j
            dve.wait_ge(ada_in[slot], i * (16 * (per // 2)) + 16 * ((j - 48) // 2 + 1))
        return nc.vector.tensor_tensor_reduce(out=w, in0=w, in1=cvec[:, :], scale=1.0,
                                              scalar=0.0, op0=ALU.mult, op1=ALU.add, accum_out=dst).then_inc(ada_done, 1)

    def dve_mod(dve, j0, n, done, gains):
        dve.wait_ge(ada_done, done)
        own_d.link(dve, nc.vector.tensor_tensor(mod[:, j0:j0 + n], mod[:, j0:j0 + n],
                                                cols[:, COLS["ada_b"] + j0:COLS["ada_b"] + j0 + n], ALU.add))
        for use, gain in gains:
            g = cols[:, COLS[gain]:COLS[gain] + DT]
            sc = SHIFT[use] + DT
            last = nc.vector.scalar_tensor_tensor(out=modg[:, MODG[use]:MODG[use] + DT], in0=mod[:, sc:sc + DT],
                                                  scalar=1.0, in1=g, op0=ALU.add, op1=ALU.mult)
        last.then_inc(mod_done, 1)

    def dve_squares(dve, n, k):
        if stop and n > {"gla": 0, "ffn0": 1, "mla": 2, "ffn1": 3, "sec": 5}[stop]:
            return
        if 1 <= k < DT - 1:
            dve.wait_ge(sq_ready, DT * n + k + 1)
            if k > 1:
                dve.wait_ge(acc_done, 6 * n + k - 1)
            nc.vector.tensor_tensor(rstd[:, :], nsq[:, 0, :] if k == 1 else rstd[:, :], nsq[:, k % 4, :], ALU.add)\
              .then_inc(acc_done, 1)

    def dve_norm(dve, n):
        buf = NORM_BUF[n]
        dve.wait_ge(rs_ready, n + 1)
        if n in PLAIN:
            for k in range(DT):
                nc.vector.scalar_tensor_tensor(out=x[:, k, :], in0=x[:, k, :], scalar=col(PLAIN[n], k),
                                               in1=rstd[:, :], op0=ALU.mult, op1=ALU.mult)\
                  .then_inc(fin_ready if n == 4 else y_ready, 1)
            if n == 4:
                dve.wait_ge(fin_ready, DT)
                for k in range(1, DT - 1):
                    dve_squares(dve, 5, k)
            return
        u = H_USE[n]
        dve.wait_ge(mod_done, MOD_STAGE[n])
        for k in range(DT):
            nc.vector.scalar_tensor_tensor(out=buf[:, k, :], in0=x[:, k, :], scalar=modg[:, MODG[n] + k:MODG[n] + k + 1],
                                           in1=rstd[:, :], op0=ALU.mult, op1=ALU.mult).then_inc(t_ready, 1)
        for k in range(DT):
            dve.wait_ge(hh_ready, DT * u + k + 1)
            nc.vector.scalar_tensor_tensor(out=h_lo[:, k, :], in0=buf[:, k, :],
                                           scalar=mod[:, SHIFT[n] + k:SHIFT[n] + k + 1],
                                           in1=h_hi[:, k, :].bitcast(F32), op0=ALU.add, op1=ALU.subtract).then_inc(h_ready, 1)

    def dve_residual(dve, name, blocks, n, norm):
        m, T = M0[name], T0[name]
        dve.wait_ge(tile_free, T)
        if name == "sec_out":
            dve.wait_ge(fin_ready, DT)
        for k in range(DT):
            dve.wait_ge(blk_done, m + blocks * (k + 1))
            nc.vector.scalar_tensor_tensor(out=x[:, k, :], in0=ps[:, (T + k) % RING, :],
                                           scalar=mod[:, GATE[n] + k:GATE[n] + k + 1], in1=x[:, k, :],
                                           op0=ALU.mult, op1=ALU.add).then_inc(tile_free, 1)
            dve_squares(dve, norm, k - 1)

    def dve_gla(dve):
        nc.vector.memset(g_attn[:, :, :], 0.0)
        dve.wait_ge(cvec_done, 1)
        for j in range(16):
            dve_ada(dve, j, 0, mod[:, j:j + 1])
            dve_squares(dve, 0, j - 1)
        dve.wait_ge(ld_c, 32)
        dve_mod(dve, 0, 16, 16, [(0, "norm_mix0")])
        dve_norm(dve, 0)
        for j in range(16, 48):
            dve_ada(dve, j, 0, mod[:, j:j + 1])
        dve_mod(dve, 16, 32, 48, [(1, "norm_ffn0")])
        dve.wait_ge(ld_m, 64)
        for t in range(GH):
            dve.wait_ge(abs_done, t + 1)
            own_d.link(dve, nc.vector.tensor_scalar(g_min[:, :], pa[:, t, :], col("gla_b_gate", t), 0.0, ALU.add, ALU.min))
            dve.wait_ge(ln_done, t + 1)
            own_d.link(dve, nc.vector.tensor_tensor(g_ln[:, t, :], g_min[:, :], g_ln[:, t, :], ALU.subtract))
            nc.vector.tensor_tensor_scan(g_b[:, t, :], g_cm[:, :], g_ln[:, t, :], 0.0, ALU.mult, ALU.add)\
              .then_inc(scan_done, 1)
        dve.wait_ge(scan_done, GH)

        def gate_sums(e):
            h, l = divmod(e, LEVELS)
            s = GCH >> (l + 1)
            b = g_b[:, h, :].rearrange("p (n w) -> p n w", w=2 * s)
            E = g_E[:, e % 2, :].rearrange("p (n w) -> p n w", w=2 * s)
            ref = b[:, :, s - 1:s].to_broadcast([P, S // (2 * s), 2 * s])
            if e >= 2:
                dve.wait_ge(lv_q, e - 1)
            nc.vector.tensor_tensor(E, b, ref, ALU.subtract).then_inc(lv_d, 1)

        def scaled(n):
            h, l, e = item_level(n)
            dve.wait_ge(lv_e, e + 1)
            if e >= 2:
                dve.wait_ge(lv_mm, (e - 2) // LEVELS * (LEVELS + 1) + (e - 2) % LEVELS + 1)
            nc.vector.tensor_tensor(g_qs[:, e % 2, :], g_q[:, h, :], g_E[:, e % 2, :], ALU.mult)
            nc.vector.tensor_tensor(g_ks[:, e % 2, :], g_k[:, h, :], g_E[:, e % 2, :], ALU.mult).then_inc(lv_q, 1)

        def keep(n):
            h, l, _ = item_level(n)
            dve.wait_ge(lv_mm, n + 1)
            if n:
                dve.wait_ge(lv_cp, n)
            nc.vector.copy_predicated(g_attn[:, h, :].rearrange("p (c i) -> p c i", c=TT), bc(g_mask[:, l, :], 1, TT),
                                      pa[:, n % 4, :].rearrange("p (c i) -> p c i", c=TT)).then_inc(lv_cp, 1)

        dve.wait_ge(tile_free, 2 * GH)
        gate_sums(0)
        for n in range(ITEMS):
            h, l, e = item_level(n)
            if l < LEVELS:
                if e + 1 < GH * LEVELS:
                    gate_sums(e + 1)
                scaled(n)
            if n:
                keep(n - 1)
        keep(ITEMS - 1)
        last = g_b[:, :, :].rearrange("p h (c t) -> p h c t", c=TT)
        nc.vector.tensor_copy(g_bl[:, :, :], last[:, :, :, GCH - 1]).then_inc(dec_d, 1)
        dve.wait_ge(dec_e, 1)
        nc.vector.tensor_tensor(g_q[:, :, :], g_q[:, :, :], g_eb[:, :, :], ALU.mult).then_inc(qe_ready, 1)
        dve.wait_ge(dec_d, 1)
        for h in range(GH):
            tail = nc.vector.tensor_tensor(last[:, h, :, :], bc(g_bl[:, h, :], 2, GCH), last[:, h, :, :], ALU.subtract)
        tail.then_inc(dec_d, 1)
        dve.wait_ge(dec_e, 3)
        nc.vector.tensor_tensor(g_k[:, :, :], g_k[:, :, :], g_b[:, :, :], ALU.mult).then_inc(qe_ready, 1)
        for c in range(TT - 1):
            dve.wait_ge(st_mm, c + 1)
            if c:
                dve.wait_ge(st_out, c)
            for h in range(GH):
                new = ps[:, h // 2, GDV * (h % 2):GDV * (h % 2 + 1)]
                if c:
                    tail = nc.vector.scalar_tensor_tensor(out=g_S[:, h, :], in0=g_S[:, h, :], scalar=g_dec[:, h, c:c + 1],
                                                          in1=new, op0=ALU.mult, op1=ALU.add)
                else:
                    tail = nc.vector.tensor_copy(g_S[:, h, :], new)
            tail.then_inc(st_out, 1)
        for k in range(DT):
            if k == 0:
                dve.wait_ge(r_silu, 1)
            if k >= R_CHUNKS:
                dve.wait_ge(tile_free, T0["gla_r"] + k + 1)
            dve.wait_ge(oq_ready, k + 1)
            nc.vector.scalar_tensor_tensor(out=g_o[:, k, :], in0=g_o[:, k, :], scalar=col("gla_g_out", k % 2),
                                           in1=g_r[:, k, :], op0=ALU.mult, op1=ALU.mult).then_inc(og_ready, 1)
        dve.wait_ge(ors_ready, 1)
        for k in range(DT):
            dve.wait_ge(og_ready, k + 1)
            nc.vector.tensor_tensor(g_o[:, k, :], g_o[:, k, :], g_rs[:, k // 2, :], ALU.mult).then_inc(ot_ready, 1)
        for k in range(DT):
            dve.wait_ge(oh_hi, k + 1)
            nc.vector.tensor_tensor(h_lo[:, k, :], g_o[:, k, :], h_hi[:, k, :].bitcast(F32), ALU.subtract).then_inc(o_ready, 1)
        dve.wait_ge(ld_x, 16)
        dve_residual(dve, "gla_out", 1, 0, 1)

    def dve_ffn(dve, l):
        m, T = M0[f"ffn{l}_in"], T0[f"ffn{l}_in"]
        j0 = 48 * (l + 1)
        dve.wait_ge(tile_free, T)
        dve.wait_ge(cvec_done, l + 1)

        def two_products(i):
            for q in range(2):
                dve.wait_ge(sil_done, i * 2 + (FT * l + q + 1))
                dve.wait_ge(blk_done, i * 4 + (m + 2 * q + 2))
                if l or q or not isinstance(i, int):
                    dve.wait_ge(f_ready, i * 2 + (FT * l + q))
                nc.vector.tensor_tensor(f_pr[:, :], f_sg[:, q, :], ps[:, (T + 2 * q + 1) % RING, :], ALU.mult)\
                    .then_inc(tile_free, 2)
                dve.wait_ge(tile_free, i * 4 + (T + 2 * q + 2))
                nc.vector.tensor_copy(f_hi[:, bass.ds(i * 2 + q, 1), :], f_pr[:, :].unsqueeze(1)).then_inc(fh_ready, 1)
                dve.wait_ge(fh_ready, i * 2 + (FT * l + q + 1))
                nc.vector.tensor_tensor(f_lo[:, bass.ds(i * 2 + q, 1), :], f_pr[:, :].unsqueeze(1),
                                        f_hi[:, bass.ds(i * 2 + q, 1), :].bitcast(F32), ALU.subtract).then_inc(f_ready, 1)
                for k in range(2 * q, 2 * q + 2):
                    if not isinstance(i, int):
                        dve_ada(dve, (i, j0 + k - 2, 4), k % 2, ada4[:, k:k + 1])
                    elif q:
                        dve_ada(dve, j0 + k - 2, k % 2, mod[:, j0 + k - 2:j0 + k - 1])
            if not isinstance(i, int):
                dve.wait_ge(ada_done, i * 4 + (j0 + 2))
                nc.vector.tensor_copy(mod[:, bass.ds(i * 4 + (j0 - 2), 4)], ada4[:, 0:4]).then_inc(ada_out, 1)
                dve.wait_ge(ada_out, i + (FT // 2 - 1) * l)

        two_products(0)
        with dve.Fori(1, FT // 2) as i:
            two_products(i)
        for k in range(2 * FT - 2, 48):
            dve_ada(dve, j0 + k, k % 2, mod[:, j0 + k:j0 + k + 1])
        if l == 0:
            dve_mod(dve, 48, 48, 96, [(2, "norm_mix1"), (3, "norm_ffn1")])
        else:
            dve_mod(dve, 96, 48, 144, [(5, "norm1"), (6, "norm2")])
        dve_residual(dve, f"ffn{l}_out", 3, 2 * l + 1, 2 * l + 2)

    TWO_PI = 2 * np.pi
    C1 = 6.28125
    C2 = float(np.float32(np.floor((TWO_PI - C1) * 2 ** 21) / 2 ** 21))
    C3 = float(np.float32(TWO_PI - C1 - C2))
    MAGIC = 1.5 * 2 ** 23
    PI_BELOW = 3.1415925

    def dve_mla(dve):
        def step(ins):
            own_d.link(dve, ins)

        v = nc.vector
        dve.wait_ge(ld_v[2], 16)
        step(v.tensor_copy(m_ang[:, :], m_pos[:, :]))
        step(v.tensor_scalar(m_ang[:, :], m_ang[:, :], const("freq", 1), None, ALU.mult))
        step(v.tensor_scalar(m_t[:, :], m_ang[:, :], 1.0 / TWO_PI, MAGIC, ALU.mult, ALU.add))
        step(v.tensor_scalar(m_t[:, :], m_t[:, :], -MAGIC, None, ALU.add))
        for c in (C1, C2, C3):
            step(v.scalar_tensor_tensor(out=m_ang[:, :], in0=m_t[:, :], scalar=-c, in1=m_ang[:, :], op0=ALU.mult, op1=ALU.add))
        step(v.tensor_scalar(m_t[:, :], m_ang[:, :], np.pi / 2, None, ALU.add))
        step(v.tensor_scalar(m_cos[:, :], m_t[:, :], PI_BELOW, -TWO_PI, ALU.is_gt, ALU.mult))
        step(v.tensor_tensor(m_t[:, :], m_t[:, :], m_cos[:, :], ALU.add))
        step(v.tensor_scalar(m_t[:, :], m_t[:, :], PI_BELOW, -PI_BELOW, ALU.min, ALU.max))
        v.tensor_scalar(m_ang[:, :], m_ang[:, :], PI_BELOW, -PI_BELOW, ALU.min, ALU.max).then_inc(ang_done, 1)
        dve.wait_ge(c_rs, 1)
        dve.wait_ge(tile_free, T0["mla_in"] + 5)
        for t in range(5):
            g = col("mla_g_q", t) if t < 3 else col("mla_g_kv", t - 3)
            v.scalar_tensor_tensor(out=m_c[:, t, :], in0=m_c[:, t, :], scalar=g, in1=m_rs[:, int(t >= 3), :],
                                   op0=ALU.mult, op1=ALU.mult).then_inc(c_t, 1)
            if t:
                dve.wait_ge(c_h, t)
                v.tensor_tensor(c_lo[:, t - 1, :], m_c[:, t - 1, :], c_hi[:, t - 1, :].bitcast(F32), ALU.subtract).then_inc(c_rd, 1)
        dve.wait_ge(c_h, 5)
        v.tensor_tensor(c_lo[:, 4, :], m_c[:, 4, :], c_hi[:, 4, :].bitcast(F32), ALU.subtract).then_inc(c_rd, 1)
        dve.wait_ge(trig_done, 1)
        dve.wait_ge(tile_free, T0["mla_qn"])
        step(v.tensor_tensor(m_kr[:, :], m_kraw[:, :], m_cos[:, :], ALU.mult))
        step(v.tensor_tensor(m_sw[:, :], m_sw[:, :], m_sin[:, :], ALU.mult))
        v.tensor_tensor(m_kr[:, :], m_kr[:, :], m_sw[:, :], ALU.add).then_inc(kr_done, 1)
        T = T0["mla_qr"]
        for j in range(MH // 2):
            dve.wait_ge(blk_done, M0["mla_q"] + 4 + j // 2 + 1)
            dve.wait_ge(sw_done, 4 * (j + 1))
            sw = (m_sw, m_kraw)[j % 2]
            v.tensor_tensor(m_qr[:, j, :], m_cos[:, :], ps[:, (T + j) % RING, :], ALU.mult).then_inc(tile_free, 1)
            step(v.tensor_tensor(sw[:, :], sw[:, :], m_sin[:, :], ALU.mult))
            dve.wait_ge(tile_free, T + j + 1)
            v.tensor_tensor(m_qr[:, j, :], m_qr[:, j, :], sw[:, :], ALU.add).then_inc(qr_done, 1)
        n_it = MH * TT
        for s in range(n_it + 4):
            if s < n_it:
                dve.wait_ge(at_s, s + 1)
                step(v.tensor_reduce(m_st[:, s, 0:1], pa[:, s % 3, 0:P * (s % TT + 1)], AX.X, ALU.max))
                v.tensor_scalar(m_st[:, s, 1:2], m_st[:, s, 0:1], -MSCALE, None, ALU.mult).then_inc(at_m, 1)
            if 1 <= s <= n_it:
                r = s - 1
                dve.wait_ge(at_p, s)
                step(v.reciprocal(m_st[:, r, 3:4], m_st[:, r, 2:3]))
                pr = m_P[:, r % 2, 0:P * (r % TT + 1)]
                v.tensor_scalar(pr, pr, m_st[:, r, 3:4], None, ALU.mult).then_inc(at_n, 1)
            if s >= 7 and (s - 7) % TT == 0:
                h = (s - 7) // TT
                dve.wait_ge(at_oh, h + 1)
                v.tensor_tensor(h_lo[:, h, :], ps[:, 2 + h % 2, :], h_hi[:, h, :].bitcast(F32), ALU.subtract).then_inc(at_ol, 1)
        dve_residual(dve, "mla_out", 1, 2, 3)

    def dve_second(dve):
        v = nc.vector

        def step(ins):
            own_d.link(dve, ins)

        v.memset(s_gl[:, :, 0:PAD], 0.0)
        v.memset(s_p[:, :, 0:PPAD], 0.0)
        step(v.memset(s_pb[:, :, 0:PPAD], 0.0))
        for t in range(4):
            dve.wait_ge(tile_free, T0["sec_a2"] + t + 1)
            v.tensor_tensor(s_gl[:, t, PAD:], s_a1[:, t, :], s_sig[:, :], ALU.mult).then_inc(glu_done, 1)
        dve.wait_ge(glu_done, 4)
        for t in range(4):
            v.tensor_scalar(s_acc[:, t, :], s_gl[:, t, 0:S], col("dw_kernel", t * CK), col("dw_bias", t),
                            ALU.mult, ALU.add).then_inc(conv_done, 1)
        with dve.Fori(0, CK - 1) as i:
            for t in range(4):
                dve.wait_ge(conv_done, i * 4 + (t + 1))
                v.scalar_tensor_tensor(out=s_acc[:, t, :], in0=s_gl[:, t, bass.ds(i + 1, S)],
                                       scalar=cols[:, bass.ds(i + (COLS["dw_kernel"] + t * CK + 1), 1)],
                                       in1=s_acc[:, t, :], op0=ALU.mult, op1=ALU.add).then_inc(conv_done, 1)
        for g, w in enumerate(WINDOWS):
            dve.wait_ge(tile_free, T0["sec_p"] + g + 1)
            if g:
                dve.wait_ge(mix_done, g)
            cur, d, b = s_p[:, g, :], 1, 0
            while d < w:
                step(v.tensor_tensor(s_pb[:, b, d:], cur[:, d:], cur[:, :PPAD + S - d], ALU.add))
                cur, d, b = s_pb[:, b, :], 2 * d, 1 - b
            mean0 = s_m2[:, 0:PPAD]
            step(v.tensor_tensor(mean0, cur[:, PPAD:2 * PPAD], consts[:, CONST["invcnt"] + g * PPAD:CONST["invcnt"] + (g + 1) * PPAD],
                                 ALU.mult))
            v.scalar_tensor_tensor(out=s_mix[:, g, PPAD:], in0=cur[:, 2 * PPAD:], scalar=1.0 / w, in1=s_p[:, g, 2 * PPAD:],
                                   op0=ALU.mult, op1=ALU.subtract)
            v.tensor_tensor(s_mix[:, g, 0:PPAD], mean0, s_p[:, g, PPAD:2 * PPAD], ALU.subtract).then_inc(mix_done, 1)
        dve.wait_ge(conv_done, 4 * CK)
        dve.wait_ge(cmu, 1)
        for t in range(4):
            v.scalar_tensor_tensor(out=s_acc[:, t, :], in0=pa[:, 0, :], scalar=-1.0 / CW, in1=s_acc[:, t, :],
                                   op0=ALU.mult, op1=ALU.add).then_inc(cx, 1)
        for g in range(4):
            dve.wait_ge(pmh, g + 1)
            v.tensor_tensor(pm_lo[:, g, :], s_tmp[:, g % 2, :], pm_hi[:, g, :].bitcast(F32), ALU.subtract).then_inc(pml, 1)
        T = T0["pool_up"]
        dve.wait_ge(tile_free, T)
        for k in range(DT):
            dve.wait_ge(blk_done, M0["pool_up"] + k // 2 + 1)
            v.tensor_tensor(s_sg[:, k, :], s_sg[:, k, :], ps[:, (T + k) % RING, :], ALU.mult).then_inc(tile_free, 1)
        dve.wait_ge(crs, 1)
        dve.wait_ge(cx, 4)
        for t in range(4):
            v.scalar_tensor_tensor(out=s_acc[:, t, :], in0=s_acc[:, t, :], scalar=col("ln_g", t), in1=rstd[:, :],
                                   op0=ALU.mult, op1=ALU.mult).then_inc(ct, 1)
        for t in range(4):
            dve.wait_ge(cyh, t + 1)
            v.tensor_tensor(cy_lo[:, t, :], s_acc[:, t, :], cy_hi[:, t, :].bitcast(F32), ALU.subtract).then_inc(cyl, 1)
        T = T0["conv_out"]
        dve.wait_ge(tile_free, T)
        for k in range(DT):
            dve.wait_ge(blk_done, M0["conv_out"] + k // 2 + 1)
            v.tensor_tensor(s_m2[:, :], s_sg[:, DT + k, :], ps[:, (T + k) % RING, :], ALU.mult).then_inc(tile_free, 1)
            dve.wait_ge(tile_free, T + k + 1)
            v.tensor_tensor(s_tmp[:, k % 2, :], s_m2[:, :], s_sg[:, k, :], ALU.add).then_inc(mgt, 1)
            dve.wait_ge(mgh, k + 1)
            v.tensor_tensor(mg_lo[:, k, :], s_tmp[:, k % 2, :], mg_hi[:, k, :].bitcast(F32), ALU.subtract).then_inc(mg_done, 1)
        dve_residual(dve, "sec_out", 1, 5, 6)

    LOWEST = -3.0e38

    def dve_top16(dve, settle, vals, ix, src):
        v, lists = nc.vector, range(src.shape[1])
        for t in lists:
            last = v.max(vals[:, t, 0:8], src[:, t, :])
        settle(last)
        for t in lists:
            last = v.max_index(ix[:, t, 0:8], vals[:, t, 0:8], src[:, t, :])
        settle(last)
        for t in lists:
            last = v.match_replace(src[:, t, :], vals[:, t, 0:8], src[:, t, :], LOWEST)
        settle(last)
        for t in lists:
            last = v.max(vals[:, t, 8:16], src[:, t, :])
        settle(last)
        for t in lists:
            last = v.max_index(ix[:, t, 8:16], vals[:, t, 8:16], src[:, t, :])
        settle(last)

    def dve_router(dve):
        v = nc.vector

        def step(ins):
            own_d.link(dve, ins)

        def settle(ins):
            step(ins)
            v.tensor_copy(r_wait[:, 0:1], iota[:, 0:1])

        dve.wait_ge(rs_out, 4 * TT)
        with dve.Fori(0, TT) as i:
            own_d.begin(i, 21)
            settle(v.tensor_copy(r_w[:, :, :].unsqueeze(1), r_s[:, bass.ds(i, 1), :, :]))
            dve_top16(dve, settle, r_v, r_ix, r_w)
            settle(v.tensor_tensor(r_cand[:, :, :].rearrange("p h (a b) -> p h a b", a=TK), bc(r_v[:, 0::2, :], 3, TK),
                                 bc(r_v[:, 1::2, :], 2, TK), ALU.add))
            dve_top16(dve, settle, r_top, r_pos, r_cand)
            v.tensor_scalar(r_k[:, 0, :, :], r_pos[:, :, :], 4, None, ALU.logical_shift_right)
            step(v.tensor_scalar(r_k[:, 1, :, :], r_pos[:, :, :], TK - 1, None, ALU.bitwise_and))
            v.tensor_copy(r_kf[:, :, :, :], r_k[:, :, :, :])
            step(v.tensor_copy(r_ixf[:, :, :], r_ix[:, :, :]))
            for a in range(2):
                step(v.tensor_tensor(r_oh[:, :, :, :], bc(r_kf[:, a, :, :], 3, TK), bc(bc(iota[:, 0:TK], 1, TK), 1, PH), ALU.is_equal))
                step(v.tensor_tensor(r_oh[:, :, :, :], r_oh[:, :, :, :], bc(r_ixf[:, a::2, :], 2, TK), ALU.mult))
                step(v.tensor_reduce(r_i[:, a, bass.ds(i, 1), :].rearrange("p o (h k) -> p (o h) k", h=PH), r_oh[:, :, :, :], AX.X, ALU.add))
            step(v.tensor_tensor(r_i[:, 2, bass.ds(i, 1), :].rearrange("p o (h k) -> p (o h) k", h=PH), r_top[:, :, :],
                                 r_top[:, :, 0:1].to_broadcast([P, PH, TK]), ALU.subtract))
            own_d.end(TT)
        v.memset(r_z[:, :, :, :], 0.0).then_inc(top_done, 1)
        dve.wait_ge(gx_done, 1)
        e = r_i[:, 2, :, :].rearrange("p t (h k) -> p (t h) k", k=TK)
        z0, z1 = (r_z[:, a, :, :].rearrange("p t h -> p (t h)") for a in range(2))
        step(v.tensor_reduce(z0, e, AX.X, ALU.add))
        step(v.reciprocal(z1, z0))
        v.tensor_tensor(e, e, bc(z1, 2, TK), ALU.mult).then_inc(gate_done, 1)
        dve.wait_ge(rt_done, 3)
        v.tensor_tensor(r_T[:, 3, :], pa[:, 2, :], r_T[:, 2, :], ALU.subtract).then_inc(rt_done, 1)
        dve.wait_ge(rt_done, 4)
        per = 2 * WTOK // 4
        with dve.Fori(0, S // (2 * WTOK)) as i:
            for g in range(per):
                dve.wait_ge(wb_mm, i * per + (g + 1))
                for j in range(4):
                    s = g % 2 * 4 + j
                    tok = i * (2 * WTOK) + (4 * g + j)
                    key1, key2, ghi, glo = (r_T[:, a, bass.ds(tok, 1)] for a in range(4))
                    v.tensor_scalar(oh_ahi[:, s, :], iota, key1, ghi, ALU.is_equal, ALU.mult)
                    v.tensor_scalar(oh_alo[:, s, :], iota, key1, glo, ALU.is_equal, ALU.mult)
                    ins = v.tensor_scalar(oh_b[:, s, :], iota, key2, None, ALU.is_equal)
                ins.then_inc(oh_ready, 1)

    def dve_peer(dve):
        v = nc.vector
        dve_router(dve)
        m, T = M0["expert_v"], T0["expert_v"]
        dve.wait_ge(wb_mm, 2 + S // 4)

        def gated(g, k, b, i=None):
            def val(n, per):
                return n if i is None else i * per + n

            if k == 0:
                dve.wait_ge(e_w_in, val(16 * (g + 1), 32))
                if g >= 2 or i is not None:
                    dve.wait_ge(blk_done, val(m + GE * (g - 1), 2 * GE))
            dve.wait_ge(e_g_in[k % 4], val(16 * (g * GE // 4 + k // 4 + 1), 16 * 2 * GE // 4))
            if g or k:
                dve.wait_ge(wa_done, val(GE * g + k, 2 * GE))
            v.tensor_tensor(e_t[:, :].rearrange("p (t k) -> p t k", k=WTOK), e_g[:, k % 4, :].rearrange("p (t k) -> p t k", k=WTOK),
                            e_w[:, :, k, :], ALU.mult).then_inc(wa_t, 1)
            dve.wait_ge(wa_h, val(GE * g + k + 1, 2 * GE))
            v.tensor_tensor(wa_lo[:, b, k, :], e_t[:, :], wa_hi[:, b, k, :].bitcast(F32), ALU.subtract).then_inc(wa_done, 1)

        def add(g, k, i=None):
            dve.wait_ge(blk_done, m + GE * g + k + 1 if i is None else i * (2 * GE) + (m + GE * g + k + 1))
            if g or i is not None:
                dve.wait_ge(tile_free, T + DT * (g - 1) + k + 1 if i is None else i * (2 * DT) + (T + DT * (g - 1) + k + 1))
            v.scalar_tensor_tensor(out=x[:, k, :], in0=ps[:, (T + k) % RING, :], scalar=mod[:, GATE[6] + k:GATE[6] + k + 1],
                                   in1=x[:, k, :], op0=ALU.mult, op1=ALU.add).then_inc(tile_free, 1)

        for k in range(GE):
            gated(0, k, 0)
        dve.wait_ge(tile_free, T)
        with dve.Fori(0, NG // 2 - 1) as i:
            for g in range(2):
                for k in range(GE):
                    gated(g + 1, k, (g + 1) % 2, i)
                    add(g, k, i)
        for k in range(GE):
            gated(NG - 1, k, 1)
            add(NG - 2, k)
        for k in range(GE):
            add(NG - 1, k)
            dve_squares(dve, 7, k - 1)

    def dve_program(dve):
        dve_gla(dve)
        if stop == "gla":
            return
        dve_norm(dve, 1)
        dve_ffn(dve, 0)
        if stop == "ffn0":
            return
        dve_norm(dve, 2)
        dve_mla(dve)
        if stop == "mla":
            return
        dve_norm(dve, 3)
        dve_ffn(dve, 1)
        if stop == "ffn1":
            return
        dve_norm(dve, 4)
        dve.wait_ge(fin_ready, DT)
        dve_norm(dve, 5)
        dve_second(dve)
        if stop == "sec":
            return
        dve_norm(dve, 6)
        dve_peer(dve)
        dve_norm(dve, 7)

    MSCALE = float((NOPE + ROPE) ** -0.5)

    def mm(out, a, b, start, stop_):
        return nc.tensor.matmul(out, a, b, start=start, stop=stop_)

    def unit(out, slot, c, hi, lo, start, stop_):
        wh, wl = w_hi[:, slot, c:c + P], w_lo[:, slot, c:c + P]
        mm(out, wh, hi, start, False)
        mm(out, wh, lo, False, False)
        return mm(out, wl, hi, False, stop_)

    def turned(out, slot, c, n, hi, lo, start, stop_):
        wh, wl = w_hi[:, slot, c:c + n], w_lo[:, slot, c:c + n]
        mm(out, hi, wh, start, False)
        mm(out, hi, wl, False, False)
        return mm(out, lo, wh, False, stop_)

    def pe_norm(pe, n):
        if n == 0:
            pe.wait_ge(ld_c, 32)
        pe.wait_ge(acc_done, 6 * (n + 1))
        mm(pa[:, 0, :], ones, rstd[:, :], True, False)
        pe.wait_ge(sq_ready, DT * (n + 1))
        mm(pa[:, 0, :], ones, nsq[:, 3, :], False, True).then_inc(ss_done, 1)

    def pe_block(pe, m, i=None, per=0):
        pe.wait_ge(lo_done, m + 1 if i is None else i * per + (m + 1))

    def pe_bank(pe, T, i=None, per=0):
        if T >= RING:
            pe.wait_ge(tile_free, T - (RING - 1) if i is None else i * per + (T - (RING - 1)))
        return ps[:, T % RING, :]

    def pe_pair(pe, m, T, hi, lo, hi_ready, lo_ready):
        outs = []
        for t in range(2):
            pe_block(pe, m + t)
            outs.append(pe_bank(pe, T + t))
        for k in range(DT):
            pe.wait_ge(hi_ready[0], hi_ready[1] + k + 1)
            for t in range(2):
                mm(outs[t], w_hi[:, (m + t) % RING, k * P:(k + 1) * P], hi[:, k, :], k == 0, False)
                mm(outs[t], w_lo[:, (m + t) % RING, k * P:(k + 1) * P], hi[:, k, :], False, False)
        for k in range(DT):
            pe.wait_ge(lo_ready[0], lo_ready[1] + k + 1)
            for t in range(2):
                last = mm(outs[t], w_hi[:, (m + t) % RING, k * P:(k + 1) * P], lo[:, k, :], False, k == DT - 1)
                if k == DT - 1:
                    last.then_inc(blk_done, 1)

    def pe_tiles(pe, name, tname, hi, lo, ready=None, n=None, skip=0):
        m, T = M0[name] + skip, T0[tname]
        if ready:
            pe_pair(pe, m, T, hi, lo, *ready)
        for t in range(2 if ready else 0, n or dict(TILES)[tname]):
            pe_block(pe, m + t)
            out = pe_bank(pe, T + t)
            for k in range(DT):
                last = unit(out, (m + t) % RING, k * P, hi[:, k, :], lo[:, k, :], k == 0, k == DT - 1)
            last.then_inc(blk_done, 1)

    def h_parts(u):
        return (hh_ready, DT * u), (h_ready, DT * u)

    def pe_gla(pe):
        pe_tiles(pe, "gla_qk", "gla_q", h_hi, h_lo, h_parts(0))
        pe_tiles(pe, "gla_qk", "gla_k", h_hi, h_lo, None, skip=GH)
        pe_tiles(pe, "gla_glr", "gla_glr", h_hi, h_lo, None)
        pe.wait_ge(tile_free, T0["gla_v"])
        pe.wait_ge(ld_m, 64)
        for t in range(GH):
            mm(pa[:, t, :], g_wg[0:GLR, t * P:(t + 1) * P], g_glr[0:GLR, :], True, True).then_inc(z_done, 1)

        taken = [0]

        def items(n):
            while taken[0] < n:
                a = taken[0]
                h, l, e = item_level(a)
                if a == 0:
                    pe.wait_ge(scan_done, GH)
                if a >= 4:
                    pe.wait_ge(lv_cp, a - 3)
                if l < LEVELS:
                    pe.wait_ge(lv_q, e + 1)
                for c in range(TT):
                    w = slice(c * GCH, (c + 1) * GCH)
                    kk, qq = (g_ks[:, e % 2, w], g_qs[:, e % 2, w]) if l < LEVELS else (g_k[:, h, w], g_q[:, h, w])
                    last = mm(pa[:, a % 4, w], kk, qq, True, True)
                last.then_inc(lv_mm, 1)
                taken[0] += 1

        def r_tile(b):
            m = M0["gla_r"] + b
            pe_block(pe, m)
            out = pe_bank(pe, T0["gla_r"] + b)
            for k in range(DT):
                last = unit(out, m % RING, k * P, h_hi[:, k, :], h_lo[:, k, :], k == 0, k == DT - 1)
            last.then_inc(blk_done, 1)

        for b in range(8 + R_ITEMS):
            m = M0["gla_v"] + b
            if b < 8:
                pe_block(pe, m)
                for t in range(TT):
                    out = pe_bank(pe, T0["gla_v"] + b // 4 * 4 + t) if b % 4 == 0 else ps[:, (T0["gla_v"] + t) % RING, :]
                    for q in range(2):
                        k = 2 * (b % 4) + q
                        w = slice(t * P, (t + 1) * P)
                        last = turned(out, m % RING, 512 * q, 512, h_hi[:, k, w], h_lo[:, k, w], k == 0, k == DT - 1)
                last.then_inc(blk_done, 1)
            else:
                r_tile(b - 8)
            items(items_by(b))
        items(ITEMS)
        for b in range(R_ITEMS, R_CHUNKS):
            r_tile(b)
        pe.wait_ge(tile_free, T0["gla_r"] + R_CHUNKS)
        pe.wait_ge(lv_cp, ITEMS)
        pe.wait_ge(qe_ready, 2)
        for c in range(TT):
            w = slice(c * GCH, (c + 1) * GCH)
            if c < TT - 1:
                if c >= 2:
                    pe.wait_ge(kt_out, c - 1)
                for h in range(GH):
                    last = nc.tensor.transpose(ps[:, 2 + c % 2, h * P:(h + 1) * P], g_k[:, h, w], ident)
                last.then_inc(kt_mm, 1)
            if c >= 2:
                pe.wait_ge(o_out, 2 * (c - 1))
            if c:
                pe.wait_ge(st_out, c)
            for h in range(GH):
                for a in range(2):
                    out = pa[:, 2 * (c % 2) + a, h * GCH:(h + 1) * GCH]
                    d = slice(a * P, (a + 1) * P)
                    last = mm(out, g_v[:, c, h * GDV + a * P:h * GDV + (a + 1) * P], g_attn[:, h, w], True, c == 0)
                    if c:
                        last = mm(out, g_S[:, h, d], g_q[:, h, w], False, True)
            last.then_inc(o_mm, 1)
            if c < TT - 1:
                pe.wait_ge(kt_out, c + 1)
                for h in range(GH):
                    last = mm(ps[:, h // 2, GDV * (h % 2):GDV * (h % 2 + 1)], g_kT[:, c % 2, h, :],
                              g_v[:, c, h * GDV:(h + 1) * GDV], True, True)
                last.then_inc(st_mm, 1)
        pe.wait_ge(o_out, 2 * TT)
        for k in range(DT):
            pe.wait_ge(oq_ready, k + 1)
            last = mm(pa[:, k // 2, :], ones, nsq[:, k % 4, :], k % 2 == 0, k % 2 == 1)
            if k % 2 == 1:
                last.then_inc(oss_done, 1)
        pe.wait_ge(st_out, TT - 1)
        pe.wait_ge(kt_out, TT - 1)
        for b in range(R_CHUNKS, DT):
            r_tile(b)
        pe_tiles(pe, "gla_out", "gla_out", h_hi, h_lo, ((oh_hi, 0), (o_ready, 0)))

    def pe_ffn(pe, l):
        u = H_USE[2 * l + 1]
        m, T = M0[f"ffn{l}_in"], T0[f"ffn{l}_in"]

        def four(i, t0):
            for t in range(t0, 4):
                pe_block(pe, m + t, i, 4)
                out = pe_bank(pe, T + t, i, 4)
                for k in range(DT):
                    last = unit(out, (m + t) % RING, k * P, h_hi[:, k, :], h_lo[:, k, :], k == 0, k == DT - 1)
                last.then_inc(blk_done, 1)

        pe_pair(pe, m, T, h_hi, h_lo, *h_parts(u))
        four(0, 2)
        with pe.Fori(1, FT // 2) as i:
            four(i, 0)
        m, T = M0[f"ffn{l}_out"], T0[f"ffn{l}_out"]
        pe.wait_ge(f_ready, FT * (l + 1))
        with pe.Fori(0, 2) as i:
            for t in range(4):
                out = pe_bank(pe, T + t, i, 4)
                f = 0
                for b, n in enumerate(FSPLIT):
                    mb = m + 3 * t + b
                    pe_block(pe, mb, i, 12)
                    for q in range(n):
                        last = unit(out, mb % RING, q * P, f_hi[:, f, :], f_lo[:, f, :], f == 0, f == FT - 1)
                        f += 1
                    last.then_inc(blk_done, 1)

    def pe_mla(pe):
        pe_tiles(pe, "mla_in", "mla_in", h_hi, h_lo, h_parts(2))
        for t in range(5):
            pe.wait_ge(c_sq, t + 1)
            last = mm(pa[:, 1 if t < 3 else 2, :], ones, msq[:, t, :], t in (0, 3), t in (2, 4))
        last.then_inc(c_ss, 1)
        for t in range(12):
            m, T = M0["mla_q"] + t // 2, T0["mla_qn"] + t
            if t % 2 == 0:
                pe_block(pe, m)
            if t == 0:
                pe.wait_ge(c_rd, 3)
            out = pe_bank(pe, T)
            for k in range(3):
                last = unit(out, m % RING, (t % 2 * 3 + k) * P, c_hi[:, k, :], c_lo[:, k, :], k == 0, k == 2)
            if t % 2 == 1:
                last.then_inc(blk_done, 1)
        pe.wait_ge(c_rd, 5)
        for t in range(MH):
            m, T = M0["mla_k"] + t // 4, T0["mla_k"] + t
            if t % 4 == 0:
                pe_block(pe, m)
            out = pe_bank(pe, T)
            for k in range(2):
                last = unit(out, m % RING, (t % 4 * 2 + k) * P, c_hi[:, 3 + k, :], c_lo[:, 3 + k, :], k == 0, k == 1)
            if t % 4 == 3:
                last.then_inc(blk_done, 1)
        for c in range(2):
            m = M0["mla_v"] + c
            pe_block(pe, m)
            for t in range(TT):
                out = pe_bank(pe, T0["mla_v"] + 4 * c + t)
                for k in range(2):
                    w = slice(t * P, (t + 1) * P)
                    last = turned(out, m % RING, 512 * k, 512, c_hi[:, 3 + k, w], c_lo[:, 3 + k, w], k == 0, k == 1)
            last.then_inc(blk_done, 1)
        pe.wait_ge(tile_free, T0["mla_out"])
        pe.wait_ge(qr_done, MH // 2)
        pe.wait_ge(kr_done, 1)
        n_it = MH * TT
        for s in range(n_it + 3):
            if s < n_it:
                h, qb = divmod(s, TT)
                if s >= 3:
                    pe.wait_ge(at_p, s - 2)
                n, q = P * (qb + 1), slice(qb * P, (qb + 1) * P)
                half = slice(ROPE * (h % 2), ROPE * (h % 2 + 1))
                mm(pa[:, s % 3, 0:n], m_qn[:, h, q], m_kn[:, h, 0:n], True, False)
                mm(pa[:, s % 3, 0:n], m_qr[half, h // 2, q], m_kr[half, 0:n], False, False)
                mm(pa[:, s % 3, n - P:n], ident, const("causal_t", P), False, True).then_inc(at_s, 1)
            if 2 <= s < n_it + 2:
                r = s - 2
                pe.wait_ge(at_n, r + 1)
                if r >= 2:
                    pe.wait_ge(at_To, r - 1)
                for kb in range(r % TT + 1):
                    last = nc.tensor.transpose(ps[:, r % 2, kb * P:(kb + 1) * P], m_P[:, r % 2, kb * P:(kb + 1) * P], ident)
                last.then_inc(at_T, 1)
            if s >= 6 and (s - 6) % TT == 0:
                h = (s - 6) // TT
                pe.wait_ge(at_To, TT * (h + 1))
                if h >= 2:
                    pe.wait_ge(at_ol, h - 1)
                for kb in range(TT):
                    last = mm(ps[:, 2 + h % 2, kb * P:S], m_v[:, kb, h * MVD:(h + 1) * MVD], m_PT[:, h % 2, kb, kb * P:S],
                              kb == 0, kb == TT - 1)
                last.then_inc(at_o, 1)
        pe.wait_ge(at_ol, MH)
        pe_tiles(pe, "mla_out", "mla_out", h_hi, h_lo, None)

    def pe_second(pe):
        pe_tiles(pe, "sec_in", "sec_a1", h_hi, h_lo, h_parts(4), n=28)
        pe.wait_ge(ld_m, 80)
        for g in range(4):
            pe.wait_ge(mix_done, g + 1)
            if g >= 2:
                pe.wait_ge(pmh, g - 1)
            mm(pa[:, 2 + g % 2, :], s_pw[:, g, :], s_mix[:, g, :], True, True).then_inc(pw_mm, 1)
        pe.wait_ge(conv_done, 4 * CK)
        for t in range(4):
            last = mm(pa[:, 0, :], ones, s_acc[:, t, :], t == 0, t == 3)
        last.then_inc(cmu, 1)

        def branch(name, hi, lo):
            for k in range(DT):
                mk, T = M0[name] + k // 2, T0[name] + k
                if k % 2 == 0:
                    pe_block(pe, mk)
                out = pe_bank(pe, T)
                for q in range(4):
                    last = unit(out, mk % RING, (k % 2 * 4 + q) * P, hi[:, q, :], lo[:, q, :], q == 0, q == 3)
                if k % 2 == 1:
                    last.then_inc(blk_done, 1)

        pe.wait_ge(csq, 4)
        for t in range(4):
            last = mm(pa[:, 1, :], ones, s_csq[:, t, :], t == 0, t == 3)
        last.then_inc(cvar, 1)
        pe.wait_ge(pml, 4)
        branch("pool_up", pm_hi, pm_lo)
        pe.wait_ge(cyl, 4)
        branch("conv_out", cy_hi, cy_lo)
        pe_tiles(pe, "sec_out", "sec_out", mg_hi, mg_lo, ((mgh, 0), (mg_done, 0)))

    def pe_peer(pe):
        pe_tiles(pe, "query", "query", h_hi, h_lo, h_parts(5))
        pe.wait_ge(tile_free, T0["expert_u"])
        for t in range(TT):
            for b in range(4):
                if t:
                    pe.wait_ge(rs_out, 4 * (t - 1) + b + 1)
                for a in range(4):
                    q = 4 * b + a
                    last = mm(pa[:, b, a * NK:(a + 1) * NK], r_q[:, q, t * P:(t + 1) * P], keys[:, q % 2, :], True, True)
                last.then_inc(rs_mm, 1)

        def first(m, T, k, i, per):
            pe_block(pe, m + k, i, per)
            out = pe_bank(pe, T + k, i, per)
            for d in range(DT):
                last = unit(out, (m + k) % RING, d * P, h_hi[:, d, :], h_lo[:, d, :], d == 0, d == DT - 1)
            last.then_inc(blk_done, 1)

        m, T = M0["expert_u"], T0["expert_u"]
        with pe.Fori(0, U_FIRST // RING) as i:
            for k in range(RING):
                first(m, T, k, i, RING)
        pe.wait_ge(gate_done, 1)
        pe.wait_ge(rs_out, 4 * TT)
        for a in range(3):
            for t in range(TT):
                last = nc.tensor.transpose(pa[:, a, t * P:(t + 1) * P], r_i[:, a, t, :], ident)
                if a == t == 0:
                    last.then_inc(wb_mm, 2)
        last.then_inc(rt_mm, 1)
        m, T = m + U_FIRST, T + U_FIRST
        with pe.Fori(0, S // WTOK // 2) as i:
            for k in range(WPER):
                first(m, T, k, i, WPER)
                n = 2 * WTOK // 4 // WPER
                for g in range(n * k, n * k + n):
                    pe.wait_ge(oh_ready, i * (2 * WTOK // 4) + (g + 1))
                    pe.wait_ge(wb_free, i * (2 * WTOK // 4) + (g + 1))
                    for j in range(4):
                        s, out = g % 2 * 4 + j, pa[:, g % 4, j * NK:(j + 1) * NK]
                        mm(out, oh_b[:, s, :], oh_ahi[:, s, :], True, False)
                        last = mm(out, oh_b[:, s, :], oh_alo[:, s, :], False, True)
                    last.then_inc(wb_mm, 1)
        m, T = m + U_GATES, T + U_GATES
        with pe.Fori(0, U_LAST // RING) as i:
            for k in range(RING):
                first(m, T, k, i, RING)
        m, T = M0["expert_v"], T0["expert_v"]
        with pe.Fori(0, NG // 2) as i:
            for g in range(2):
                pe.wait_ge(wa_done, i * (2 * GE) + GE * (g + 1))
                for k in range(DT):
                    n = GE * g + k
                    pe_block(pe, m + n, i, 2 * GE)
                    out = pe_bank(pe, T + n, i, 2 * GE)
                    for e in range(GE):
                        last = unit(out, (m + n) % RING, e * P, wa_hi[:, g, e, :], wa_lo[:, g, e, :], e == 0, e == GE - 1)
                    last.then_inc(blk_done, 1)

    def pe_program(pe):
        pe_norm(pe, 0)
        pe_gla(pe)
        if stop == "gla":
            return
        pe_norm(pe, 1)
        pe_ffn(pe, 0)
        if stop == "ffn0":
            return
        pe_norm(pe, 2)
        pe_mla(pe)
        if stop == "mla":
            return
        pe_norm(pe, 3)
        pe_ffn(pe, 1)
        if stop == "ffn1":
            return
        pe_norm(pe, 4)
        pe_norm(pe, 5)
        pe_second(pe)
        if stop == "sec":
            return
        pe_norm(pe, 6)
        pe_peer(pe)
        pe_norm(pe, 7)

    with nc.Block() as block:
        @block.sync
        def _(sp):
            sp_program(sp)
            if stop is not None:
                sp.wait_ge(lo_done, HI_END)
                sp.wait_ge(tile_free, DT + T0[{"gla": "gla_out", "ffn0": "ffn0_out", "mla": "mla_out", "ffn1": "ffn1_out", "sec": "sec_out"}[stop]])
            for k in range(DT):
                if stop is None:
                    sp.wait_ge(y_ready, k + 1)
                sp.dma_start(out[k, :, :], x[:, k, :]).then_inc(st_out_done, 16)
            sp.wait_ge(st_out_done, 16 * DT)

        @block.gpsimd
        def _(pool):
            pool_program(pool)

        @block.scalar
        def _(act):
            act_program(act)

        @block.vector
        def _(dve):
            dve_program(dve)

        @block.tensor
        def _(pe):
            pe_program(pe)


def units_of(w):
    k, n = w.shape
    return w.reshape(k // P, P, n // P, P).transpose(2, 1, 0, 3).reshape(n // P, P, k)


def rows_of(w, per):
    k, n = w.shape
    return w.reshape(k // P // per, per, P, n // 512, 512).transpose(3, 0, 2, 1, 4).reshape(-1, P, per * 512)


def columns(v):
    return v.reshape(-1, P).T


def joined(blocks, n):
    b, p, c = blocks.shape
    return blocks.reshape(b // n, n, p, c).transpose(0, 2, 1, 3).reshape(b // n, p, n * c)


def lay_out(i):
    a = {}
    a["x"] = i["x"][0].T.reshape(DT, P, S)
    a["c"], a["c_2"], a["positions"] = i["c"][0], i["c_2"][0], i["positions"][0]
    ada = np.concatenate([i["ada_w"], i["ada_w_2"]])
    a["ada"] = ada.transpose(0, 2, 1).reshape(144, P, D)
    a["cols"] = np.concatenate(
        [columns(np.concatenate([i["ada_b"], i["ada_b_2"]]).reshape(-1))]
        + [columns(v) for v in (i["norm_mix"][0], i["norm_mix"][1], i["norm_ffn"][0], i["norm_ffn"][1], i["final_norm"],
                                i["norm1_g_2"][0], i["norm2_g_2"][0], i["final_g_2"], i["gla_b_gate"][0], i["gla_g_out"][0],
                                i["mla_g_q"][0], i["mla_g_kv"][0], i["b_in_2"][0], i["pool_scale_2"][0], i["dw_bias_2"][0],
                                i["conv_ln_g_2"][0], i["conv_ln_b_2"][0])]
        + [i["dw_kernel_2"][0].reshape(CK, 4, P).transpose(2, 1, 0).reshape(P, 4 * CK)], axis=1)
    a["consts"] = make_consts()
    a["masks"] = make_level_masks().reshape(P, -1)
    a["chunk_mask"] = make_chunk_mask()
    a["keys"] = np.concatenate([i["sub_keys_1_2"][0].T, i["sub_keys_2_2"][0].T], axis=1)
    g = i["gla_w_in"][0]
    nq, nv = GH * GDK, GH * GDV
    a["gla_qk"] = units_of(g[:, 0:2 * nq])
    a["gla_glr"] = units_of(np.tile(g[:, 2 * nq + 2 * nv:], (1, P // GLR)))[0]
    a["gla_v"] = rows_of(g[:, 2 * nq:2 * nq + nv], 2)
    a["gla_r"] = units_of(g[:, 2 * nq + nv:2 * nq + 2 * nv])
    a["gla_w_gate"] = i["gla_w_gate"][0]
    a["gla_out"] = units_of(i["gla_w_out"][0])
    for l in range(2):
        w = units_of(i["ffn_w_in"][l])
        a[f"ffn{l}_in"] = w.reshape(2, FT, P, D).transpose(1, 0, 2, 3).reshape(2 * FT, P, D)
        a[f"ffn{l}_out"] = units_of(i["ffn_w_out"][l])
    halves = np.concatenate([np.arange(0, ROPE, 2), np.arange(1, ROPE, 2)])
    w = i["mla_w_in"][0]
    kr = w[:, QR + KVR:][:, halves]
    a["mla_in"] = units_of(np.concatenate([w[:, :QR + KVR], kr, kr], axis=1))
    q = i["mla_w_q_up"][0].reshape(QR, MH, NOPE + ROPE)
    q = np.concatenate([q[:, :, :NOPE].reshape(QR, -1), q[:, :, NOPE:][:, :, halves].reshape(QR, -1)], axis=1)
    a["mla_q"] = joined(units_of(q), 2)
    kv = i["mla_w_kv_up"][0].reshape(KVR, MH, NOPE + MVD)
    a["mla_k"] = joined(units_of(kv[:, :, :NOPE].reshape(KVR, -1)), 4)
    a["mla_v"] = rows_of(kv[:, :, NOPE:].reshape(KVR, -1), 2)
    a["mla_out"] = units_of(i["mla_w_out"][0])
    w = i["w_in_2"][0]
    a["sec_in"] = units_of(np.concatenate([w[:, PW:PW + 2 * CW], w[:, :PW], w[:, PW + 2 * CW:]], axis=1))
    a["pool_w"] = i["pool_w_2"][0]
    a["pool_up"] = joined(units_of(i["pool_up_2"][0]), 2)
    a["conv_out"] = joined(units_of(i["conv_out_2"][0]), 2)
    a["sec_out"] = units_of(i["w_out_2"][0])
    a["query"] = units_of(i["w_query_2"][0])
    a["expert_u"] = units_of(i["expert_u_2"][0].T)
    a["expert_v"] = i["expert_v_2"][0].reshape(NG, GE, P, DT, P).transpose(0, 3, 2, 1, 4).reshape(NG * DT, P, GE * P)
    return {k: np.ascontiguousarray(v) for k, v in a.items()}


def build(nc, arrays, stop=None):
    A = {n: nc.dram_tensor(f"in_{n}", a.shape, mybir.dt.from_np(a.dtype), kind="ExternalInput").ap() for n, a in arrays.items()}
    out = nc.dram_tensor("out", (DT, P, S), F32, kind="ExternalOutput").ap()
    two_blocks(nc, A, out, stop)


def kernel(**inputs):
    import concourse.bacc as bacc
    from concourse.bass_utils import run_bass_kernel_spmd

    arrays = lay_out({k: np.asarray(v) for k, v in inputs.items()})
    nc = bacc.Bacc("TRN2", target_bir_lowering=False, num_devices=1)
    build(nc, arrays)
    r = run_bass_kernel_spmd(nc, [{f"in_{n}": a for n, a in arrays.items()}], core_ids=[0])
    got = r.results[0]["out"]
    return np.ascontiguousarray(np.asarray(got).reshape(D, S).T)[None]
```
